# Optimizing a Trainium2 kernel written in Bass

```python
import math
import jax, jax.numpy as jnp
from jax import lax
import numpy as np
import jax
import jax.numpy as jnp

D_MODEL = 1024
BATCH = 1
SEQ = 256
DEPTH = 2

PLE_DIM = 256
MIX_WIDTH = D_MODEL
RET_HEAD_DIM = 128
RET_HEADS = (MIX_WIDTH // 2) // RET_HEAD_DIM
RET_WIDTH = RET_HEADS * RET_HEAD_DIM
MOBA_HEAD_DIM = 128
MOBA_HEADS = (MIX_WIDTH - RET_WIDTH) // MOBA_HEAD_DIM
MOBA_WIDTH = MOBA_HEADS * MOBA_HEAD_DIM
SPLIT_SIZES = [RET_WIDTH] * 4 + [MOBA_WIDTH] * 4
IN_WIDTH = sum(SPLIT_SIZES)
RET_CHUNK = 128
MOBA_BLOCK = 256
MOBA_TOPK = 3
MOBA_Q_CHUNK = 64
N_BUCKETS = 32
MAX_DISTANCE = 2048
ROPE_THETA = 10000.0
EPS = 1e-6
NEG_INF = -1e30


def rms_norm(x, g=None):
    xf = x.astype(jnp.float32)
    y = xf * lax.rsqrt(jnp.mean(xf * xf, axis=-1, keepdims=True) + EPS)
    if g is not None:
        y = y * g.astype(jnp.float32)
    return y.astype(x.dtype)

def rotary(x, pos):
    half = x.shape[-1] // 2
    inv = ROPE_THETA ** (-jnp.arange(half, dtype=jnp.float32) / half)
    ang = pos.astype(jnp.float32)[:, None] * inv[None, :]
    cos = jnp.cos(ang)[None, :, None, :]
    sin = jnp.sin(ang)[None, :, None, :]
    x1, x2 = x[..., :half], x[..., half:]
    return jnp.concatenate([x1 * cos - x2 * sin, x1 * sin + x2 * cos], axis=-1)

def t5_bucket(n):
    max_exact = N_BUCKETS // 2
    nf = jnp.maximum(n, 1).astype(jnp.float32)
    large = max_exact + (jnp.log(nf / max_exact) / math.log(MAX_DISTANCE / max_exact)
                         * (N_BUCKETS - max_exact)).astype(jnp.int32)
    large = jnp.minimum(large, N_BUCKETS - 1)
    return jnp.where(n < max_exact, n, large)

def retention(q, k, v, gain):
    B, S, H, d = q.shape
    C = RET_CHUNK
    nc = S // C
    log_g = jnp.log1p(-jnp.power(2.0, -5.0 - jnp.arange(H, dtype=jnp.float32)))

    def chunks(t):
        return t.reshape(B, nc, C, H, d).transpose(0, 3, 1, 2, 4)

    qc, kc, vc = chunks(q), chunks(k * (d ** -0.5)), chunks(v)
    j = jnp.arange(C, dtype=jnp.float32)
    rel = j[:, None] - j[None, :]
    decay = jnp.where(rel >= 0, jnp.exp(log_g[:, None, None] * jnp.maximum(rel, 0.0)[None]), 0.0)
    s = jnp.einsum('bhcnd,bhcmd->bhcnm', qc, kc) * decay[None, :, None]
    inner = jnp.einsum('bhcnm,bhcme->bhcne', s, vc)
    k_dec = kc * jnp.exp(log_g[:, None] * (C - 1 - j)[None])[None, :, None, :, None]
    kv = jnp.einsum('bhcmd,bhcme->cbhde', k_dec, vc)
    chunk_decay = jnp.exp(log_g * C)[None, :, None, None]

    def step(state, kv_c):
        return state * chunk_decay + kv_c, state

    _, prev = lax.scan(step, jnp.zeros((B, H, d, d), jnp.float32), kv)
    q_dec = qc * jnp.exp(log_g[:, None] * (j + 1.0)[None])[None, :, None, :, None]
    cross = jnp.einsum('bhcnd,cbhde->bhcne', q_dec, prev)
    o = (inner + cross).transpose(0, 2, 3, 1, 4).reshape(B, S, H, d)
    mu = jnp.mean(o, axis=-1, keepdims=True)
    var = jnp.mean(jnp.square(o - mu), axis=-1, keepdims=True)
    o = (o - mu) * lax.rsqrt(var + EPS)
    return o.reshape(B, S, H * d) * gain.astype(jnp.float32)

def moba(q, k, v, rel_bias):
    B, S, H, d = q.shape
    BLK, QC = MOBA_BLOCK, MOBA_Q_CHUNK
    nb = -(-S // BLK)
    pad = nb * BLK - S
    q = q.transpose(0, 2, 1, 3) * (d ** -0.5)
    kp = jnp.pad(k.transpose(0, 2, 1, 3), ((0, 0), (0, 0), (0, pad), (0, 0)))
    vp = jnp.pad(v.transpose(0, 2, 1, 3), ((0, 0), (0, 0), (0, pad), (0, 0)))
    kb = kp.reshape(B, H, nb, BLK, d)
    vb = vp.reshape(B, H, nb, BLK, d)
    kmean = jnp.mean(kb, axis=3)

    qpos = jnp.arange(S)
    qblock = qpos // BLK
    gate = jnp.einsum('bhsd,bhnd->bhsn', q, kmean)
    past = jnp.arange(nb)[None, :] < qblock[:, None]
    gate = jnp.where(past[None, None], gate, NEG_INF)
    n_sel = min(MOBA_TOPK, nb)
    _, top_idx = lax.top_k(gate, n_sel)

    nq = S // QC
    qx = q.reshape(B, H, nq, QC, d).transpose(2, 0, 1, 3, 4)
    ix = top_idx.reshape(B, H, nq, QC, n_sel).transpose(2, 0, 1, 3, 4)
    bi = jnp.arange(B)[:, None, None, None]
    hi = jnp.arange(H)[None, :, None, None]
    offs = jnp.arange(BLK)
    bias_h = rel_bias.astype(jnp.float32).T

    def one_chunk(args):
        c, qc, ic = args
        qp = c * QC + jnp.arange(QC)
        qblk = (c * QC) // BLK
        ksel = kb[bi, hi, ic]
        vsel = vb[bi, hi, ic]
        kpos = ic[..., None] * BLK + offs
        dist = qp[None, None, :, None, None] - kpos
        ok = (ic < qblk)[..., None]
        s_sel = (jnp.einsum('bhqd,bhqnkd->bhqnk', qc, ksel)
                 + bias_h[hi[..., None], t5_bucket(jnp.maximum(dist, 0))])
        s_sel = jnp.where(ok, s_sel, NEG_INF).reshape(B, H, QC, n_sel * BLK)
        kown = lax.dynamic_index_in_dim(kb, qblk, axis=2, keepdims=False)
        vown = lax.dynamic_index_in_dim(vb, qblk, axis=2, keepdims=False)
        dist_own = qp[:, None] - (qblk * BLK + offs)[None, :]
        s_own = (jnp.einsum('bhqd,bhkd->bhqk', qc, kown)
                 + bias_h[:, t5_bucket(jnp.maximum(dist_own, 0))][None])
        s_own = jnp.where(dist_own >= 0, s_own, NEG_INF)
        pr = jax.nn.softmax(jnp.concatenate([s_sel, s_own], axis=-1), axis=-1)
        p_sel = pr[..., :n_sel * BLK].reshape(B, H, QC, n_sel, BLK)
        p_own = pr[..., n_sel * BLK:]
        return (jnp.einsum('bhqnk,bhqnkd->bhqd', p_sel, vsel)
                + jnp.einsum('bhqk,bhkd->bhqd', p_own, vown))

    out = lax.map(one_chunk, (jnp.arange(nq), qx, ix))
    return out.transpose(1, 0, 3, 2, 4).reshape(B, S, H * d)

def first_inputs(seed: int = 0) -> dict:
    key = jax.random.key(seed)
    ks = jax.random.split(key, 12)
    f = jnp.float32
    nrm = jax.random.normal
    return {
        "x": nrm(ks[0], (BATCH, SEQ, D_MODEL), f),
        "p": nrm(ks[1], (DEPTH, BATCH, SEQ, PLE_DIM), f),
        "norm_g": 1.0 + 0.02 * nrm(ks[2], (DEPTH, D_MODEL), f),
        "w_in": nrm(ks[3], (DEPTH, D_MODEL, IN_WIDTH), f) * D_MODEL ** -0.5,
        "ret_norm_g": 1.0 + 0.02 * nrm(ks[4], (DEPTH, RET_WIDTH), f),
        "q_norm_g": 1.0 + 0.02 * nrm(ks[5], (DEPTH, MOBA_HEAD_DIM), f),
        "k_norm_g": 1.0 + 0.02 * nrm(ks[6], (DEPTH, MOBA_HEAD_DIM), f),
        "rel_bias": 0.5 * nrm(ks[7], (N_BUCKETS, MOBA_HEADS), f),
        "w_out": nrm(ks[8], (DEPTH, MIX_WIDTH, D_MODEL), f) * MIX_WIDTH ** -0.5,
        "w_ple": nrm(ks[9], (DEPTH, PLE_DIM, D_MODEL), f) * PLE_DIM ** -0.5,
        "ple_norm_g": 1.0 + 0.02 * nrm(ks[10], (DEPTH, D_MODEL), f),
        "w_ple_gate": nrm(ks[11], (DEPTH, D_MODEL, D_MODEL), f) * D_MODEL ** -0.5,
    }

def first_block(x, p, norm_g, w_in, ret_norm_g, q_norm_g, k_norm_g, rel_bias,
              w_out, w_ple, ple_norm_g, w_ple_gate):
    B, S, _ = x.shape
    f32 = jnp.float32
    pos = jnp.arange(S)
    cuts = list(np.cumsum(SPLIT_SIZES)[:-1])

    def heads(t, H):
        return t.astype(f32).reshape(B, S, H, -1)

    for i in range(DEPTH):
        h = rms_norm(x, norm_g[i])
        proj = h @ w_in[i]
        rq, rk, rv, rz, mq, mk, mv, mz = jnp.split(proj, cuts, axis=-1)
        r_out = retention(rotary(heads(rq, RET_HEADS), pos), rotary(heads(rk, RET_HEADS), pos),
                          heads(rv, RET_HEADS), ret_norm_g[i])
        r_out = jax.nn.silu(rz.astype(f32)) * r_out
        q_m = rms_norm(heads(mq, MOBA_HEADS), q_norm_g[i])
        k_m = rms_norm(heads(mk, MOBA_HEADS), k_norm_g[i])
        m_out = moba(q_m, k_m, heads(mv, MOBA_HEADS), rel_bias)
        m_out = jax.nn.silu(mz.astype(f32)) * m_out
        y = jnp.concatenate([r_out, m_out], axis=-1).astype(x.dtype) @ w_out[i]
        x = x + y
        gate = jax.nn.sigmoid((rms_norm(x) @ w_ple_gate[i]).astype(f32))
        e = rms_norm(p[i] @ w_ple[i], ple_norm_g[i]).astype(f32)
        x = x + (gate * e).astype(x.dtype)
    return x


N_EVEN = (DEPTH + 1) // 2
N_ODD = DEPTH // 2
N_VRES = max(N_EVEN - 1, 0)

MIX_HALF = D_MODEL // 2

RW_WIDTH = MIX_HALF
RW_HEAD_DIM = 64
RW_HEADS = RW_WIDTH // RW_HEAD_DIM
RW_DECAY_RANK = 64
RW_ICLR_RANK = 64
RW_GATE_RANK = 128
RW_VRES_RANK = 32
RW_SHIFT_COLS = 3 * RW_WIDTH + RW_DECAY_RANK + RW_ICLR_RANK + RW_GATE_RANK
RW_SPLITS = (RW_WIDTH, 2 * RW_WIDTH, 3 * RW_WIDTH, 3 * RW_WIDTH + RW_DECAY_RANK,
             3 * RW_WIDTH + RW_DECAY_RANK + RW_ICLR_RANK)
RW_LN_EPS = 64e-5

POOL_WIDTH = MIX_HALF
POOL_WINDOWS = (2, 4, 8, 16)
POOL_GROUPS = len(POOL_WINDOWS)
POOL_GROUP_DIM = POOL_WIDTH // POOL_GROUPS

EVEN_IN = RW_SHIFT_COLS + POOL_WIDTH
EVEN_MIX = RW_WIDTH + POOL_WIDTH

DA_WIDTH = MIX_HALF
DA_HEAD_DIM = 64
DA_VALUE_DIM = 2 * DA_HEAD_DIM
DA_HEADS = DA_WIDTH // DA_VALUE_DIM
DA_QK_COLS = DA_HEADS * 2 * DA_HEAD_DIM
Q_BLOCK = 128
SUBLN_EPS = 1e-5

S5_WIDTH = MIX_HALF
S5_GROUP_DIM = 16
S5_GROUPS = S5_WIDTH // S5_GROUP_DIM
S5_STATE = 64

ODD_IN = 2 * DA_QK_COLS + DA_WIDTH + S5_WIDTH
ODD_MIX = DA_WIDTH + S5_WIDTH

MOE_GROUPS = 4
MOE_EXPERTS_PER_GROUP = 8
MOE_EXPERTS = MOE_GROUPS * MOE_EXPERTS_PER_GROUP
MOE_TOP_K = 2
MOE_HIDDEN = D_MODEL // 2
MOE_BLOCK = 128

RMS_EPS = 1e-6


def rms_norm_2(x, g, eps=RMS_EPS):
    xf = x.astype(jnp.float32)
    y = xf * lax.rsqrt(jnp.mean(xf * xf, axis=-1, keepdims=True) + eps)
    return (y * g.astype(jnp.float32)).astype(x.dtype)

def token_shift(u):
    return jnp.pad(u, ((0, 0), (1, 0), (0, 0)))[:, :-1]

def rwkv7_recurrence(r, w, k, v, a, b):
    bsz, _, n_heads, n = r.shape
    seq = tuple(jnp.moveaxis(t.astype(jnp.float32), 1, 0) for t in (r, w, k, v, a, b))

    def step(state, inp):
        r_t, w_t, k_t, v_t, a_t, b_t = inp
        sa = jnp.einsum('bhij,bhj->bhi', state, a_t)
        state = (state * w_t[:, :, None, :] + sa[..., None] * b_t[:, :, None, :]
                 + v_t[..., None] * k_t[:, :, None, :])
        return state, jnp.einsum('bhij,bhj->bhi', state, r_t)

    s0 = jnp.zeros((bsz, n_heads, n, n), jnp.float32)
    _, y = lax.scan(step, s0, seq)
    return jnp.moveaxis(y, 0, 1)

def multiscale_pool(u, pool_w, pool_scale):
    bsz, t_len, _ = u.shape
    uf = u.astype(jnp.float32).reshape(bsz, t_len, POOL_GROUPS, POOL_GROUP_DIM)
    csum = jnp.cumsum(uf, axis=1)
    n_seen = jnp.arange(1, t_len + 1, dtype=jnp.float32)
    diffs = []
    for gi, win in enumerate(POOL_WINDOWS):
        c = csum[:, :, gi]
        lagged = jnp.pad(c, ((0, 0), (win, 0), (0, 0)))[:, :t_len]
        mean = (c - lagged) / jnp.minimum(n_seen, float(win))[None, :, None]
        diffs.append(mean - uf[:, :, gi])
    d = jnp.stack(diffs, axis=2).astype(u.dtype)
    y = jnp.einsum('btgc,gcd->btgd', d, pool_w)
    return y.reshape(bsz, t_len, POOL_WIDTH) * pool_scale

def even_mixer(h, v_first, w_in, mu, w0, w2, a0, a2, g2, k_k, k_a, r_k, ln_g, ln_b, vres,
               pool_w, pool_scale, w_out):
    bsz, t_len, _ = h.shape
    u = h @ w_in
    u_rw, u_pool = u[..., :RW_SHIFT_COLS], u[..., RW_SHIFT_COLS:]
    m = u_rw + (token_shift(u_rw) - u_rw) * mu
    r, k, v, dw, da, dg = jnp.split(m, RW_SPLITS, axis=-1)
    w = -jax.nn.softplus(-(w0 + jnp.tanh(dw) @ w2)) - 0.5
    decay = jnp.exp(-jnp.exp(w.astype(jnp.float32)))
    a = jax.nn.sigmoid(a0 + da @ a2)
    g = jax.nn.sigmoid(dg) @ g2
    if v_first is None:
        v_first = v
    else:
        v0, v1, v2 = vres
        v = v + (v_first - v) * jax.nn.sigmoid(v0 + (v @ v1) @ v2)

    def heads(t):
        return t.reshape(bsz, t_len, RW_HEADS, RW_HEAD_DIM)

    kk = heads(k * k_k).astype(jnp.float32)
    kk = kk / jnp.maximum(jnp.sqrt(jnp.sum(kk * kk, axis=-1, keepdims=True)), 1e-12)
    k = k * (1.0 + (a - 1.0) * k_a)
    rh, kh, vh, ah = heads(r), heads(k), heads(v), heads(a)
    y = rwkv7_recurrence(rh, heads(decay), kh, vh, -kk, kk * ah.astype(jnp.float32))
    mean = jnp.mean(y, axis=-1, keepdims=True)
    var = jnp.mean(jnp.square(y - mean), axis=-1, keepdims=True)
    y = ((y - mean) * lax.rsqrt(var + RW_LN_EPS)).reshape(bsz, t_len, RW_WIDTH)
    y = (y * ln_g + ln_b).astype(h.dtype)
    bonus = jnp.sum(rh * kh * r_k, axis=-1, keepdims=True) * vh
    o_rw = (y + bonus.reshape(bsz, t_len, RW_WIDTH)) * g
    o_pool = multiscale_pool(u_pool, pool_w, pool_scale)
    return jnp.concatenate([o_rw, o_pool], axis=-1) @ w_out, v_first

def rope_tables(t_len, dim):
    inv_freq = ROPE_THETA ** (-jnp.arange(0, dim, 2, dtype=jnp.float32) / dim)
    ang = jnp.arange(t_len, dtype=jnp.float32)[:, None] * inv_freq[None, :]
    return jnp.cos(ang), jnp.sin(ang)

def apply_rope(x, cos, sin):
    xf = x.astype(jnp.float32)
    x1, x2 = jnp.split(xf, 2, axis=-1)
    c = cos[:, None, None, :]
    s = sin[:, None, None, :]
    return jnp.concatenate([x1 * c - x2 * s, x2 * c + x1 * s], axis=-1).astype(x.dtype)

def diff_attention(q, k, v, lam):
    t_len = q.shape[1]
    scale = DA_HEAD_DIM ** -0.5
    pos = jnp.arange(t_len)
    outs = []
    for s in range(0, t_len, Q_BLOCK):
        e = s + Q_BLOCK
        sc = jnp.einsum('bqhmd,bkhmd->bhmqk', q[:, s:e], k[:, :e]).astype(jnp.float32) * scale
        mask = pos[s:e, None] >= pos[None, :e]
        p = jax.nn.softmax(jnp.where(mask, sc, -jnp.inf), axis=-1)
        attn = p[:, :, 0] - lam * p[:, :, 1]
        outs.append(jnp.einsum('bhqk,bkhd->bqhd', attn.astype(v.dtype), v[:, :e]))
    return jnp.concatenate(outs, axis=1)

def s5_mixer(u, a_re, a_im, log_step, b_re, b_im, c_re, c_im, d_skip, w_glu):
    bsz, t_len, _ = u.shape
    f32 = jnp.float32
    uf = u.astype(f32).reshape(bsz, t_len, S5_GROUPS, S5_GROUP_DIM)
    lam = lax.complex(jnp.minimum(a_re.astype(f32), -1e-4), a_im.astype(f32))
    step = jnp.exp(log_step.astype(f32))
    lam_bar = jnp.exp(lam * step)
    b_bar = ((lam_bar - 1.0) / lam)[..., None] * lax.complex(b_re.astype(f32), b_im.astype(f32))
    c_mat = lax.complex(c_re.astype(f32), c_im.astype(f32))
    bu = jnp.einsum('gpc,btgc->btgp', b_bar, uf.astype(jnp.complex64))
    a_seq = jnp.broadcast_to(lam_bar, bu.shape)

    def combine(left, right):
        a_l, b_l = left
        a_r, b_r = right
        return a_r * a_l, a_r * b_l + b_r

    _, states = lax.associative_scan(combine, (a_seq, bu), axis=1)
    y = jnp.einsum('gcp,btgp->btgc', c_mat, states).real + d_skip.astype(f32) * uf
    z = jax.nn.gelu(y.reshape(bsz, t_len, S5_WIDTH)).astype(u.dtype)
    return z * jax.nn.sigmoid(z @ w_glu)

def odd_mixer(h, layer_idx, w_in, q_norm, k_norm, lam_q1, lam_k1, lam_q2, lam_k2, subln,
              a_re, a_im, log_step, b_re, b_im, c_re, c_im, d_skip, w_glu, w_out):
    bsz, t_len, _ = h.shape
    f32 = jnp.float32
    u = h @ w_in
    q, k, v, u_s5 = jnp.split(u, (DA_QK_COLS, 2 * DA_QK_COLS, 2 * DA_QK_COLS + DA_WIDTH), axis=-1)
    q = q.reshape(bsz, t_len, DA_HEADS, 2, DA_HEAD_DIM)
    k = k.reshape(bsz, t_len, DA_HEADS, 2, DA_HEAD_DIM)
    v = v.reshape(bsz, t_len, DA_HEADS, DA_VALUE_DIM)
    cos, sin = rope_tables(t_len, DA_HEAD_DIM)
    q = apply_rope(rms_norm_2(q, q_norm), cos, sin)
    k = apply_rope(rms_norm_2(k, k_norm), cos, sin)
    lam_init = 0.8 - 0.6 * math.exp(-0.3 * layer_idx)
    lam = (jnp.exp(jnp.sum(lam_q1.astype(f32) * lam_k1.astype(f32)))
           - jnp.exp(jnp.sum(lam_q2.astype(f32) * lam_k2.astype(f32))) + lam_init)
    o = diff_attention(q, k, v, lam)
    o = rms_norm_2(o, subln, SUBLN_EPS) * (1.0 - lam_init)
    o_attn = o.reshape(bsz, t_len, DA_WIDTH)
    o_ssm = s5_mixer(u_s5, a_re, a_im, log_step, b_re, b_im, c_re, c_im, d_skip, w_glu)
    return jnp.concatenate([o_attn, o_ssm], axis=-1) @ w_out

def routed_experts(hf, expert_idx, gates, w_gate, w_up, w_down):
    n_tok, d = hf.shape
    n_slot = n_tok * MOE_TOP_K
    flat_e = expert_idx.reshape(-1)
    flat_tok = jnp.arange(n_slot, dtype=jnp.int32) // MOE_TOP_K
    flat_g = gates.reshape(-1)
    order = jnp.argsort(flat_e)
    sorted_e = flat_e[order]
    counts = jnp.bincount(flat_e, length=MOE_EXPERTS)
    padded = (counts + MOE_BLOCK - 1) // MOE_BLOCK * MOE_BLOCK
    seg_start = jnp.cumsum(counts) - counts
    cum_padded = jnp.cumsum(padded)
    pad_start = cum_padded - padded
    dest = pad_start[sorted_e] + jnp.arange(n_slot, dtype=jnp.int32) - seg_start[sorted_e]
    n_blocks = -(-n_slot // MOE_BLOCK) + MOE_EXPERTS
    n_pad = n_blocks * MOE_BLOCK
    buf_tok = jnp.full((n_pad,), n_tok, jnp.int32).at[dest].set(flat_tok[order])
    buf_gate = jnp.zeros((n_pad,), jnp.float32).at[dest].set(flat_g[order])
    block_start = jnp.arange(n_blocks, dtype=cum_padded.dtype) * MOE_BLOCK
    block_expert = jnp.minimum(jnp.searchsorted(cum_padded, block_start, side='right'),
                               MOE_EXPERTS - 1).astype(jnp.int32)
    h_pad = jnp.concatenate([hf, jnp.zeros((1, d), hf.dtype)], axis=0)

    def run_block(args):
        tok, e, gt = args
        xb = h_pad[tok]
        hidden = jax.nn.silu(xb @ w_gate[e]) * (xb @ w_up[e])
        return (hidden @ w_down[e]) * gt[:, None].astype(xb.dtype)

    ys = lax.map(run_block, (buf_tok.reshape(n_blocks, MOE_BLOCK), block_expert,
                             buf_gate.reshape(n_blocks, MOE_BLOCK)))
    out = jnp.zeros((n_tok + 1, d), hf.dtype).at[buf_tok].add(ys.reshape(n_pad, d))
    return out[:n_tok]

def hier_moe(h, w_group, b_group, w_expert, b_expert, w_gate, w_up, w_down):
    bsz, t_len, d = h.shape
    n_tok = bsz * t_len
    hf = h.reshape(n_tok, d)
    rows = jnp.arange(n_tok)
    g_logits = (hf @ w_group + b_group).astype(jnp.float32)
    g_prob = jax.nn.softmax(g_logits, axis=-1)
    g_top = jnp.argmax(g_logits, axis=-1).astype(jnp.int32)
    g_w = g_prob[rows, g_top]
    e_logits = (hf @ w_expert + b_expert).astype(jnp.float32)
    e_logits = e_logits.reshape(n_tok, MOE_GROUPS, MOE_EXPERTS_PER_GROUP)[rows, g_top]
    e_prob = jax.nn.softmax(e_logits, axis=-1)
    top_p, top_j = lax.top_k(e_prob, MOE_TOP_K)
    gates = g_w[:, None] * top_p / jnp.sum(top_p, axis=-1, keepdims=True)
    expert_idx = g_top[:, None] * MOE_EXPERTS_PER_GROUP + top_j.astype(jnp.int32)
    y = routed_experts(hf, expert_idx, gates, w_gate, w_up, w_down)
    return y.reshape(bsz, t_len, d)

def second_inputs(seed: int = 0) -> dict:
    key = jax.random.key(seed)
    keys = jax.random.split(key, 64)
    counter = [0]

    def nk():
        counter[0] += 1
        return keys[counter[0] - 1]

    f32 = jnp.float32

    def nrm(shape, scale):
        return scale * jax.random.normal(nk(), shape, f32)

    def gain(shape, base=1.0, noise=0.02):
        return base + noise * jax.random.normal(nk(), shape, f32)

    def unif(shape, lo, hi):
        return jax.random.uniform(nk(), shape, f32, lo, hi)

    d = D_MODEL
    res = (2.0 * DEPTH) ** -0.5
    return {
        'x': nrm((BATCH, SEQ, d), 1.0),
        'norm_mix_g': gain((DEPTH, d)),
        'norm_ffn_g': gain((DEPTH, d)),
        'even_w_in': nrm((N_EVEN, d, EVEN_IN), d ** -0.5),
        'rw_mu': unif((N_EVEN, RW_SHIFT_COLS), 0.0, 1.0),
        'rw_w0': unif((N_EVEN, RW_WIDTH), -6.0, -1.0),
        'rw_w2': nrm((N_EVEN, RW_DECAY_RANK, RW_WIDTH), RW_DECAY_RANK ** -0.5),
        'rw_a0': nrm((N_EVEN, RW_WIDTH), 0.1),
        'rw_a2': nrm((N_EVEN, RW_ICLR_RANK, RW_WIDTH), RW_ICLR_RANK ** -0.5),
        'rw_g2': nrm((N_EVEN, RW_GATE_RANK, RW_WIDTH), RW_GATE_RANK ** -0.5),
        'rw_k_k': gain((N_EVEN, RW_WIDTH), 0.85, 0.05),
        'rw_k_a': gain((N_EVEN, RW_WIDTH), 1.0, 0.05),
        'rw_r_k': nrm((N_EVEN, RW_HEADS, RW_HEAD_DIM), 0.1),
        'rw_ln_g': gain((N_EVEN, RW_WIDTH)),
        'rw_ln_b': nrm((N_EVEN, RW_WIDTH), 0.02),
        'rw_v0': nrm((N_VRES, RW_WIDTH), 0.1),
        'rw_v1': nrm((N_VRES, RW_WIDTH, RW_VRES_RANK), RW_WIDTH ** -0.5),
        'rw_v2': nrm((N_VRES, RW_VRES_RANK, RW_WIDTH), RW_VRES_RANK ** -0.5),
        'pool_w': nrm((N_EVEN, POOL_GROUPS, POOL_GROUP_DIM, POOL_GROUP_DIM), POOL_GROUP_DIM ** -0.5),
        'pool_scale': gain((N_EVEN, POOL_WIDTH)),
        'even_w_out': nrm((N_EVEN, EVEN_MIX, d), EVEN_MIX ** -0.5 * res),
        'odd_w_in': nrm((N_ODD, d, ODD_IN), d ** -0.5),
        'da_q_norm': gain((N_ODD, DA_HEAD_DIM)),
        'da_k_norm': gain((N_ODD, DA_HEAD_DIM)),
        'da_lam_q1': nrm((N_ODD, DA_HEAD_DIM), 0.1),
        'da_lam_k1': nrm((N_ODD, DA_HEAD_DIM), 0.1),
        'da_lam_q2': nrm((N_ODD, DA_HEAD_DIM), 0.1),
        'da_lam_k2': nrm((N_ODD, DA_HEAD_DIM), 0.1),
        'da_subln': gain((N_ODD, DA_VALUE_DIM)),
        's5_a_re': gain((N_ODD, S5_GROUPS, S5_STATE), -0.5, 0.01),
        's5_a_im': math.pi * jnp.arange(S5_STATE, dtype=f32) + nrm((N_ODD, S5_GROUPS, S5_STATE), 0.01),
        's5_log_step': unif((N_ODD, S5_GROUPS, S5_STATE), math.log(1e-3), math.log(1e-1)),
        's5_b_re': nrm((N_ODD, S5_GROUPS, S5_STATE, S5_GROUP_DIM), (2.0 * S5_GROUP_DIM) ** -0.5),
        's5_b_im': nrm((N_ODD, S5_GROUPS, S5_STATE, S5_GROUP_DIM), (2.0 * S5_GROUP_DIM) ** -0.5),
        's5_c_re': nrm((N_ODD, S5_GROUPS, S5_GROUP_DIM, S5_STATE), (2.0 * S5_STATE) ** -0.5),
        's5_c_im': nrm((N_ODD, S5_GROUPS, S5_GROUP_DIM, S5_STATE), (2.0 * S5_STATE) ** -0.5),
        's5_d': nrm((N_ODD, S5_GROUPS, S5_GROUP_DIM), 1.0),
        's5_w_glu': nrm((N_ODD, S5_WIDTH, S5_WIDTH), S5_WIDTH ** -0.5),
        'odd_w_out': nrm((N_ODD, ODD_MIX, d), ODD_MIX ** -0.5 * res),
        'moe_w_group': nrm((DEPTH, d, MOE_GROUPS), d ** -0.5),
        'moe_b_group': nrm((DEPTH, MOE_GROUPS), 0.01),
        'moe_w_expert': nrm((DEPTH, d, MOE_EXPERTS), d ** -0.5),
        'moe_b_expert': nrm((DEPTH, MOE_EXPERTS), 0.01),
        'moe_w_gate': nrm((DEPTH, MOE_EXPERTS, d, MOE_HIDDEN), d ** -0.5),
        'moe_w_up': nrm((DEPTH, MOE_EXPERTS, d, MOE_HIDDEN), d ** -0.5),
        'moe_w_down': nrm((DEPTH, MOE_EXPERTS, MOE_HIDDEN, d), MOE_HIDDEN ** -0.5 * res),
    }

def second_block(x, norm_mix_g, norm_ffn_g,
              even_w_in, rw_mu, rw_w0, rw_w2, rw_a0, rw_a2, rw_g2, rw_k_k, rw_k_a, rw_r_k,
              rw_ln_g, rw_ln_b, rw_v0, rw_v1, rw_v2, pool_w, pool_scale, even_w_out,
              odd_w_in, da_q_norm, da_k_norm, da_lam_q1, da_lam_k1, da_lam_q2, da_lam_k2, da_subln,
              s5_a_re, s5_a_im, s5_log_step, s5_b_re, s5_b_im, s5_c_re, s5_c_im, s5_d, s5_w_glu,
              odd_w_out,
              moe_w_group, moe_b_group, moe_w_expert, moe_b_expert, moe_w_gate, moe_w_up, moe_w_down):
    v_first = None
    for layer in range(DEPTH):
        i = layer // 2
        h = rms_norm_2(x, norm_mix_g[layer])
        if layer % 2 == 0:
            vres = None if v_first is None else (rw_v0[i - 1], rw_v1[i - 1], rw_v2[i - 1])
            mix, v_first = even_mixer(h, v_first, even_w_in[i], rw_mu[i], rw_w0[i], rw_w2[i],
                                      rw_a0[i], rw_a2[i], rw_g2[i], rw_k_k[i], rw_k_a[i], rw_r_k[i],
                                      rw_ln_g[i], rw_ln_b[i], vres, pool_w[i], pool_scale[i],
                                      even_w_out[i])
        else:
            mix = odd_mixer(h, layer, odd_w_in[i], da_q_norm[i], da_k_norm[i], da_lam_q1[i],
                            da_lam_k1[i], da_lam_q2[i], da_lam_k2[i], da_subln[i], s5_a_re[i],
                            s5_a_im[i], s5_log_step[i], s5_b_re[i], s5_b_im[i], s5_c_re[i],
                            s5_c_im[i], s5_d[i], s5_w_glu[i], odd_w_out[i])
        x = x + mix
        h = rms_norm_2(x, norm_ffn_g[layer])
        x = x + hier_moe(h, moe_w_group[layer], moe_b_group[layer], moe_w_expert[layer],
                         moe_b_expert[layer], moe_w_gate[layer], moe_w_up[layer], moe_w_down[layer])
    return x


def setup_inputs(seed=0):
    out = dict(first_inputs(seed))
    for name, value in second_inputs(seed + 1).items():
        if name != "x":
            out[name + "_2"] = value
    return out


def reference(
    x, p, norm_g, w_in, ret_norm_g, q_norm_g, k_norm_g, rel_bias, w_out, w_ple, ple_norm_g,
    w_ple_gate, norm_mix_g_2, norm_ffn_g_2, even_w_in_2, rw_mu_2, rw_w0_2, rw_w2_2, rw_a0_2,
    rw_a2_2, rw_g2_2, rw_k_k_2, rw_k_a_2, rw_r_k_2, rw_ln_g_2, rw_ln_b_2, rw_v0_2, rw_v1_2,
    rw_v2_2, pool_w_2, pool_scale_2, even_w_out_2, odd_w_in_2, da_q_norm_2, da_k_norm_2,
    da_lam_q1_2, da_lam_k1_2, da_lam_q2_2, da_lam_k2_2, da_subln_2, s5_a_re_2, s5_a_im_2,
    s5_log_step_2, s5_b_re_2, s5_b_im_2, s5_c_re_2, s5_c_im_2, s5_d_2, s5_w_glu_2, odd_w_out_2,
    moe_w_group_2, moe_b_group_2, moe_w_expert_2, moe_b_expert_2, moe_w_gate_2, moe_w_up_2,
    moe_w_down_2,
):
    x = first_block(
        x, p, norm_g, w_in, ret_norm_g, q_norm_g, k_norm_g, rel_bias, w_out, w_ple, ple_norm_g,
        w_ple_gate,
    )
    return second_block(
        x, norm_mix_g_2, norm_ffn_g_2, even_w_in_2, rw_mu_2, rw_w0_2, rw_w2_2, rw_a0_2, rw_a2_2,
        rw_g2_2, rw_k_k_2, rw_k_a_2, rw_r_k_2, rw_ln_g_2, rw_ln_b_2, rw_v0_2, rw_v1_2, rw_v2_2,
        pool_w_2, pool_scale_2, even_w_out_2, odd_w_in_2, da_q_norm_2, da_k_norm_2, da_lam_q1_2,
        da_lam_k1_2, da_lam_q2_2, da_lam_k2_2, da_subln_2, s5_a_re_2, s5_a_im_2, s5_log_step_2,
        s5_b_re_2, s5_b_im_2, s5_c_re_2, s5_c_im_2, s5_d_2, s5_w_glu_2, odd_w_out_2,
        moe_w_group_2, moe_b_group_2, moe_w_expert_2, moe_b_expert_2, moe_w_gate_2, moe_w_up_2,
        moe_w_down_2,
    )


_drawn_inputs = setup_inputs


def setup_inputs(seed=0):
    import zlib

    import numpy as np

    out = dict(_drawn_inputs(seed))
    spreads = {}
    factors = {'ret_norm_g': 3.928,
     'q_norm_g': 8.0,
     'k_norm_g': 8.0,
     'ple_norm_g': 3.144,
     'norm_mix_g_2': 4.44,
     'norm_ffn_g_2': 4.589,
     'rw_w2_2': 5.876,
     'rw_a0_2': 5.714,
     'rw_k_k_2': 53.288,
     'rw_k_a_2': 4.792,
     'rw_ln_g_2': 59.417,
     'rw_ln_b_2': 8.0,
     'pool_scale_2': 7.602,
     'da_q_norm_2': 44.338,
     'da_k_norm_2': 21.554,
     'da_lam_q1_2': 3.786,
     'da_lam_k1_2': 4.448,
     'da_lam_q2_2': 4.761,
     'da_lam_k2_2': 3.936,
     'da_subln_2': 64.0,
     's5_a_re_2': 64.0,
     's5_a_im_2': 64.0,
     's5_log_step_2': 64.0,
     's5_b_re_2': 64.0,
     's5_b_im_2': 64.0,
     's5_c_re_2': 64.0,
     's5_c_im_2': 64.0,
     'moe_b_group_2': 8.0,
     'moe_b_expert_2': 8.0}
    for name, (base, spread) in spreads.items():
        noise = np.random.default_rng([zlib.crc32(name.encode()), seed]).standard_normal(out[name].shape)
        drawn = base * np.exp(spread * noise) if base else spread * noise
        out[name] = jnp.asarray(drawn.astype(out[name].dtype))
    for name, factor in factors.items():
        out[name] = (out[name] * factor).astype(out[name].dtype)
    return out
```

```python
from contextlib import ExitStack

import numpy as np
import concourse.bass as bass
from concourse import mybir

P = 128
S = 256
TT = S // P
D = 1024
KT = D // P
HALF = 512
HT = HALF // P
DEPTH = 2
PLE = 256
RH = 4
BUCKETS = 32
NEG = -1e30
EPS = 1e-6
SUB_EPS = 1e-5
LN_EPS = 64e-5
RWH = 8
CH = 64
SG = 32
SP_ = 64
SC = 16
NPAIR = SG // 2
NE = 32
NG = 4
CAP = 64
HID = 512
SLOTS = 6
SW = 4096

IN_ORDER = (0, 1, 4, 5, 2, 6, 3, 7)

F32 = mybir.dt.float32
I32 = mybir.dt.int32
ALU = mybir.AluOpType
ACT = mybir.ActivationFunctionType
AX = mybir.AxisListType


def t5_bucket(n):
    exact = BUCKETS // 2
    nf = np.maximum(n, 1).astype(np.float32)
    large = exact + (np.log(nf / exact) / np.log(np.float32(2048 / exact)) * (BUCKETS - exact)).astype(np.int32)
    return np.where(n < exact, n, np.minimum(large, BUCKETS - 1))


def shape_constants():
    c = {}
    p = np.arange(P)
    t = np.arange(S)
    c["ident"] = np.eye(P)
    c["ones"] = np.ones((P, P))
    c["before"] = (p[:, None] < p[None, :]) * 1.0
    c["iota"] = np.tile(np.arange(CAP), (P, 2))
    c["iota_e"] = np.tile(np.arange(NE), (P, 1))
    c["head64"] = (p[:, None] // 64 == p[None, :] // 64) * 1.0
    same = p[:, None] // CH == p[None, :] // CH
    c["lt"] = same & (p[:, None] < p[None, :])
    c["le"] = same & (p[:, None] <= p[None, :])
    res = {k: np.asarray(v, np.float32) for k, v in c.items()}
    first = {}
    half = 64
    inv = (10000.0 ** (-np.arange(half, dtype=np.float32) / half)).astype(np.float32)
    ang = t.astype(np.float32)[None, :] * np.tile(inv, 2)[:, None]
    first["cos"] = np.cos(ang)
    first["sin"] = np.sin(ang)
    rot = np.zeros((P, P))
    rot[p[:half] + half, p[:half]] = -1.0
    rot[p[:half], p[:half] + half] = 1.0
    first["rot"] = rot
    lg = np.log1p(-np.power(2.0, -5.0 - np.arange(RH)))
    dec = np.zeros((P, RH, 3 * P))
    for h in range(RH):
        rel = t[None, :] - p[:, None]
        full = np.where(rel >= 0, np.exp(lg[h] * np.maximum(rel, 0)), 0.0) * P ** -0.5
        dec[:, h, 0:S] = full
        dec[:, h, S:] = full[:, 0:P]
    first["decay"] = dec.reshape(P, -1)
    oh = np.zeros((P, 511))
    j = np.arange(511)
    dist = 255 - j
    oh[t5_bucket(np.maximum(dist, 0)), j] = 1.0
    oh[:, dist < 0] = 0.0
    oh[BUCKETS, dist < 0] = 1.0
    first["buckets"] = oh
    even = {}
    m = np.zeros((P, TT, 4, S))
    for g, win in enumerate((2, 4, 8, 16)):
        s = np.arange(S)
        band = ((s[:, None] <= s[None, :]) & (s[:, None] > s[None, :] - win)) / np.minimum(s[None, :] + 1, win)
        full = band - np.eye(S)
        m[:, :, g, :] = full.reshape(TT, P, S).transpose(1, 0, 2)
    even["pool"] = m.reshape(P, -1)
    for lev in range(6):
        b = 2 ** lev
        blk = (p[:, None] // (2 * b) == p[None, :] // (2 * b)) & (p[:, None] // b != p[None, :] // b)
        even[f"lev{lev}"] = blk & (p[:, None] < p[None, :])
    even["reset"] = np.tile((t % CH != 0) * 1.0, (P, 1))
    odd = {}
    inv = (10000.0 ** (-np.arange(0, 64, 2, dtype=np.float32) / 64)).astype(np.float32)
    ang = t.astype(np.float32)[:, None] * inv[None, :]
    odd["cos"] = np.cos(ang).reshape(TT, P, 32).transpose(1, 0, 2).reshape(P, -1)
    odd["sin"] = np.sin(ang).reshape(TT, P, 32).transpose(1, 0, 2).reshape(P, -1)
    causal = np.where(p[None, :] > p[:, None], NEG, 0.0)
    odd["causal"] = np.concatenate([causal, 0 * causal, causal], axis=1)
    odd["time"] = np.tile(t, (P, 1))
    return res, *({k: np.asarray(v, np.float32) for k, v in d.items()} for d in (first, even, odd))


def packed(consts):
    where, at = {}, 0
    for k, v in consts.items():
        where[k] = (at, v.shape[1])
        at += v.shape[1]
    return np.ascontiguousarray(np.concatenate(list(consts.values()), axis=1)), where


class Steps:

    def __init__(self, nc, name):
        self.sem, self.n = nc.alloc_semaphore(name), 0

    def mark(self, ins):
        self.n += 1
        ins.then_inc(self.sem, 1)

    def wait(self, eng):
        eng.wait_ge(self.sem, self.n)

    def link(self, eng, ins):
        self.mark(ins)
        self.wait(eng)


class Program:
    def __init__(self, nc, A, out, wheres, ctx):
        self.nc, self.A, self.out, self.ctx = nc, A, out, ctx
        self.where_res, self.where_first, self.where_even, self.where_odd = wheres
        sb = self.sb
        self.ring = sb("weight_ring", [P, SLOTS, SW])
        self.x = sb("x", [P, TT, D])
        self.xs = sb("x_normed", [P, TT, D])
        self.hT = sb("hT", [P, KT, S])
        self.mixn = sb("mix_natural", [P, TT, D])
        self.mixT = sb("mix_transposed", [P, KT, S])
        self.res = sb("resident_constants", [P, sum(n for _, n in self.where_res.values())])
        self.arena_size = 16200
        self.arena = sb("arena", [P, self.arena_size])
        self.small = sb("small", [P, 512])
        self.ps = [ctx.enter_context(nc.psum_tensor(f"bank{b}", [P, 512], F32)) for b in range(8)]
        self.landed = [nc.alloc_semaphore(f"weights_landed_{s}") for s in range(SLOTS)]
        self.free_when = {}
        self.phase_sems = []
        self.act_steps = Steps(nc, "act_steps")
        self.dve_steps = Steps(nc, "dve_steps")
        self.pool_steps = Steps(nc, "pool_steps")
        self.chunks = []
        self.sent = 0
        self.limit = 0
        self.turns = sb("moe_turns", [P, 1], I32)
        self.moe_landed = [[nc.alloc_semaphore(f"moe{ly}_weights_landed_{s}") for s in range(SLOTS)] for ly in range(DEPTH)]
        self.out_written = nc.alloc_semaphore("out_written")

    def sb(self, name, shape, dt=F32):
        return self.ctx.enter_context(self.nc.sbuf_tensor(name, shape, dt))

    def sem(self, name):
        self.phase_sems.append(self.nc.alloc_semaphore(name))
        return self.phase_sems[-1]

    def end_phase(self):
        self.nc.clear_and_free_semaphores(self.phase_sems)
        self.nc.all_engine_barrier()
        self.phase_sems, self.free_when = [], {}

    def con(self, k):
        at, n = self.where_res[k]
        return self.res[:, at:at + n]

    def take(self, n):
        at = self.at
        self.at += n
        assert self.at <= self.arena_size, self.at
        return self.arena[:, at:at + n]

    def send(self, sp, upto):
        while self.sent < min(upto, self.limit):
            i = self.sent
            src, k, n = self.chunks[i]
            if i - SLOTS in self.free_when:
                sp.wait_ge(*self.free_when[i - SLOTS])
            dst = self.ring[:, i % SLOTS, 0:k * n].rearrange("p (k n) -> p k n", n=n)
            sp.dma_start(dst, src).then_inc(self.landed[i % SLOTS], 16)
            self.sent += 1

    def chunk(self, pe, i):
        pe.wait_ge(self.landed[i % SLOTS], 16 * (i // SLOTS + 1))
        _, k, n = self.chunks[i]
        return self.ring[:, i % SLOTS, 0:k * n].rearrange("p (k n) -> p k n", n=n)


def bank2(ps):
    return ps[:, :].rearrange("p (a t) -> p a t", a=2)


def stage_norm(g, name, gain, s_gain=None):
    nc = g.nc
    s_rms, s_root = g.sem(name + "_sumsq"), g.sem(name + "_root")
    s_xs, s_tr, s_hT = g.sem(name + "_xs"), g.sem(name + "_transposed"), g.sem(name + "_hT")
    sm = g.small
    ident = g.con("ident")

    def act(eng):
        for tt in range(TT):
            g.act_steps.mark(eng.activation(g.xs[:, tt, :], g.x[:, tt, :], ACT.Square, accum_out=sm[:, tt:tt + 1]))
        g.act_steps.wait(eng)
        eng.mul(sm[:, 2:4], sm[:, 0:2], 1.0 / D).then_inc(s_rms, 1)
        eng.wait_ge(s_rms, 2)
        eng.activation(sm[:, 6:8], sm[:, 4:6], ACT.Sqrt).then_inc(s_root, 1)

    def dve(eng):
        eng.wait_ge(s_rms, 1)
        eng.tensor_scalar(sm[:, 4:6], sm[:, 2:4], EPS, None, ALU.add).then_inc(s_rms, 1)
        eng.wait_ge(s_root, 1)
        g.dve_steps.link(eng, eng.reciprocal(sm[:, 8:10], sm[:, 6:8]))
        for tt in range(TT):
            eng.tensor_scalar(g.xs[:, tt, :], g.x[:, tt, :], sm[:, 8 + tt:9 + tt], None, ALU.mult).then_inc(s_xs, 1)
        if s_gain is not None:
            eng.wait_ge(s_gain, 16)
        for b in range(4):
            eng.wait_ge(s_tr, b + 1)
            dst = g.hT[:, 2 * b:2 * b + 2, :]
            if gain is None:
                eng.tensor_copy(dst, bank2(g.ps[b])).then_inc(s_hT, 1)
            else:
                col = gain[:, 2 * b:2 * b + 2].unsqueeze(2).to_broadcast([P, 2, S])
                eng.tensor_tensor(dst, bank2(g.ps[b]), col, ALU.mult).then_inc(s_hT, 1)

    def pe(eng):
        eng.wait_ge(s_xs, TT)
        for b in range(4):
            for kk in range(2):
                for tt in range(TT):
                    k = 2 * b + kk
                    ins = eng.transpose(g.ps[b][:, kk * S + tt * P:kk * S + tt * P + P],
                                        g.xs[:, tt, k * P:(k + 1) * P], ident)
            ins.then_inc(s_tr, 1)

    def ready(eng):
        eng.wait_ge(s_hT, 4)

    return act, dve, pe, ready


def stage_mixT(g, name, ks):
    s_tr, s_done = g.sem(name + "_transposed"), g.sem(name + "_mixT")
    ident = g.con("ident")

    def pe(eng):
        for b in range(len(ks) // 2):
            for kk in range(2):
                for tt in range(TT):
                    k = ks[2 * b + kk]
                    ins = eng.transpose(g.ps[b][:, kk * S + tt * P:kk * S + tt * P + P],
                                        g.mixn[:, tt, k * P:(k + 1) * P], ident)
            ins.then_inc(s_tr, 1)

    def act(eng):
        for b in range(len(ks) // 2):
            eng.wait_ge(s_tr, b + 1)
            k = ks[2 * b]
            eng.copy(g.mixT[:, k:k + 2, :], bank2(g.ps[b])).then_inc(s_done, 1)

    def ready(eng):
        eng.wait_ge(s_done, len(ks) // 2)

    return pe, act, ready


def project_natural(g, pe, i, lhsT, bank, tt, n):
    w = g.chunk(pe, i)
    k_all = w.shape[1]
    for k in range(k_all):
        ins = pe.matmul(bank, lhsT[:, k, tt * P:(tt + 1) * P], w[:, k, n], start=(k == 0), stop=(k == k_all - 1))
    return ins


def first_layer(g, l, c0):
    nc, A, ps = g.nc, g.A, g.ps
    n_ = f"first{l}"
    g.at = 0
    con = {}
    for k, (at, n) in g.where_first.items():
        con[k] = g.first_consts[:, at:at + n]
    gcol = g.take(KT)
    qkg = g.take(4)
    rqk = g.take(8 * S).rearrange("p (h t) -> p h t", h=8)
    rv = g.take(TT * HALF).rearrange("p (a n) -> p a n", a=TT)
    mv = g.take(TT * HALF).rearrange("p (a n) -> p a n", a=TT)
    tmp = g.take(1024)
    tmp2 = g.take(1024)
    rgain = g.take(HALF)
    pgain = g.take(D)
    ptok = g.take(TT * PLE).rearrange("p (a n) -> p a n", a=TT)
    pT = g.take(2 * S).rearrange("p (a n) -> p a n", a=2)
    sT = [g.take(384) for _ in range(2)]
    pb = [g.take(384) for _ in range(2)]
    pbT = [g.take(384) for _ in range(2)]
    sm = g.small
    ident = g.con("ident")
    raw = g.mixT
    mqk = g.xs
    mqkT = g.mixT
    s_par = g.sem(n_ + "_params_landed")
    s_prj, s_ev = g.sem(n_ + "_projected"), g.sem(n_ + "_evacuated")
    for ch in range(8):
        g.free_when[c0 + ch] = (s_prj, 2 * ch + 2)
    s_gain = g.sem(n_ + "_gain_landed")
    n_act, n_dve, n_pe, n_ready = stage_norm(g, n_ + "_in", gcol, s_gain)
    s_rot, s_rotd = g.sem(n_ + "_swapped"), g.sem(n_ + "_rotated")
    s_mean, s_root = g.sem(n_ + "_qk_mean"), g.sem(n_ + "_qk_root")
    s_qkn, s_qkt, s_qkT = g.sem(n_ + "_qk_normed"), g.sem(n_ + "_qk_transposed"), g.sem(n_ + "_qkT")
    s_s, s_sT = g.sem(n_ + "_ret_scores"), g.sem(n_ + "_ret_decayed")
    s_o, s_oe = g.sem(n_ + "_ret_out"), g.sem(n_ + "_ret_out_copied")
    s_var, s_std = g.sem(n_ + "_ret_var"), g.sem(n_ + "_ret_std")
    s_ms, s_mb = g.sem(n_ + "_moba_scores"), g.sem(n_ + "_moba_biased")
    s_p, s_pt, s_pT = g.sem(n_ + "_moba_p"), g.sem(n_ + "_moba_p_transposed"), g.sem(n_ + "_moba_pT")
    s_mo = g.sem(n_ + "_moba_out")
    o_ret = tmp.rearrange("p (a h e) -> p a h e", a=TT, h=RH)
    o_all = tmp.rearrange("p (g e) -> p g e", e=P)
    ss = sm[:, 16:32]
    qs = sm[:, 32:48]
    qr = sm[:, 48:64]
    mx, rowsum, rinv = sm[:, 64:72], sm[:, 72:80], sm[:, 80:88]
    mu, var, std, rstd = sm[:, 88:96], sm[:, 96:104], sm[:, 104:112], sm[:, 112:120]
    bias = g.moba_bias
    unit_bank = [4 + u % 4 for u in range(12)] + [4, 5, 0, 1]
    with nc.Block() as block:
        @block.sync
        def _(sp):
            sp.dma_start(gcol, A["norm_g"][l]).then_inc(s_gain, 16)
            sp.dma_start(qkg[:, 0:1], A["q_norm_g"][l].rearrange("(d o) -> d o", o=1)).then_inc(s_par, 16)
            sp.dma_start(qkg[:, 1:2], A["k_norm_g"][l].rearrange("(d o) -> d o", o=1)).then_inc(s_par, 16)
            sp.dma_start(rgain, A["ret_norm_g"][l].partition_broadcast(P)).then_inc(s_par, 16)
            sp.dma_start(pgain, A["ple_norm_g"][l].partition_broadcast(P)).then_inc(s_par, 16)
            sp.dma_start(ptok, A["p"][l, 0].rearrange("(a p) n -> p a n", p=P)).then_inc(s_par, 16)
            g.send(sp, c0 + 8 + SLOTS)

        @block.scalar
        def _(act):
            n_act(act)

            def copy_out(u):
                ch, half = IN_ORDER[u // 2], u % 2
                bank = ps[unit_bank[u]]
                act.wait_ge(s_prj, u + 1)
                if ch < 2:
                    ins = act.copy(raw[:, 4 * ch + 2 * half:4 * ch + 2 * half + 2, :], bank2(bank))
                elif ch == 2:
                    ins = act.copy(rv[:, half, :], bank[:, :])
                elif ch == 3:
                    ins = act.activation(g.mixn[:, half, 0:HALF], bank[:, :], ACT.Silu)
                elif ch < 6:
                    ins = act.copy(mqk[:, half, (ch - 4) * HALF:(ch - 3) * HALF], bank[:, :])
                elif ch == 6:
                    ins = act.copy(mv[:, half, :], bank[:, :])
                else:
                    ins = act.activation(g.mixn[:, half, HALF:D], bank[:, :], ACT.Silu)
                ins.then_inc(s_ev, 1)

            def moba_exps(h):
                act.wait_ge(s_mb, h + 1)
                for tt in range(TT):
                    seg = slice(0, P) if tt == 0 else slice(P, 3 * P)
                    act.activation(pb[h % 2][:, seg], pb[h % 2][:, seg], ACT.Exp, bias=mx[:, 2 * h + tt:2 * h + tt + 1],
                                   accum_out=rowsum[:, 2 * h + tt:2 * h + tt + 1]).then_inc(s_p, 1)

            for u in range(12):
                copy_out(u)
            act.wait_ge(s_mean, 1)
            act.activation(qr, qs, ACT.Sqrt).then_inc(s_root, 1)
            for b in range(4):
                act.wait_ge(s_qkt, b + 1)
                act.activation(mqkT[:, 2 * b:2 * b + 2, :], bank2(ps[b]), ACT.Copy,
                               scale=qkg[:, 2 if b < 2 else 1:3 if b < 2 else 2]).then_inc(s_qkT, 1)
            copy_out(12)
            copy_out(13)
            act.wait_ge(s_o, RH)
            for tt in range(TT):
                act.copy(tmp[:, tt * HALF:(tt + 1) * HALF], ps[6 + tt][:, :]).then_inc(s_oe, 1)
            moba_exps(0)
            copy_out(14)
            act.wait_ge(s_var, 1)
            act.activation(std, var, ACT.Sqrt).then_inc(s_std, 1)
            copy_out(15)
            for h in range(RH):
                if h:
                    moba_exps(h)
                act.wait_ge(s_pt, h + 1)
                act.copy(pbT[h % 2], ps[2 + h % 2][:, 0:384]).then_inc(s_pT, 1)

        @block.vector
        def _(dve):
            link = g.dve_steps.link
            n_dve(dve)
            dve.wait_ge(s_par, 80)
            for b in range(4):
                two = slice(2 * b, 2 * b + 2)
                t1 = tmp[:, 0:512].rearrange("p (a t) -> p a t", a=2)
                t2 = tmp[:, 512:1024].rearrange("p (a t) -> p a t", a=2)
                dve.wait_ge(s_rot, b + 1)
                g.dve_steps.mark(dve.tensor_tensor(t1, raw[:, two, :], con["cos"].unsqueeze(1).to_broadcast([P, 2, S]), ALU.mult))
                link(dve, dve.tensor_tensor(t2, bank2(ps[b]), con["sin"].unsqueeze(1).to_broadcast([P, 2, S]), ALU.mult))
                dve.tensor_tensor(rqk[:, two, :], t1, t2, ALU.add).then_inc(s_rotd, 1)
                dve.wait_ge(s_rotd, b + 1)
            dve.wait_ge(s_ev, 8)
            for tt in range(TT):
                link(dve, dve.tensor_tensor(tmp, mqk[:, tt, :], mqk[:, tt, :], ALU.mult))
                link(dve, dve.tensor_reduce(ss[:, 8 * tt:8 * tt + 8], o_all, AX.X, ALU.add))
            dve.tensor_scalar(qs, ss, 1.0 / P, EPS, ALU.mult, ALU.add).then_inc(s_mean, 1)
            g.dve_steps.mark(dve.tensor_scalar(qkg[:, 2:3], qkg[:, 0:1], P ** -0.5, None, ALU.mult))
            dve.wait_ge(s_root, 1)
            link(dve, dve.reciprocal(ss, qr))
            for tt in range(TT):
                v = mqk[:, tt, :].rearrange("p (g e) -> p g e", e=P)
                dve.tensor_tensor(v, v, ss[:, 8 * tt:8 * tt + 8].unsqueeze(2).to_broadcast([P, 8, P]), ALU.mult)\
                   .then_inc(s_qkn, 1)
            for h in range(RH):
                dve.wait_ge(s_s, h + 1)
                if h >= 2:
                    dve.wait_ge(s_o, h - 1)
                dve.tensor_tensor(sT[h % 2], ps[h % 2][:, 0:384], con["decay"][:, h * 384:(h + 1) * 384], ALU.mult)\
                   .then_inc(s_sT, 1)
            def biased(h):
                dve.wait_ge(s_ms, h + 1)
                if h >= 2:
                    dve.wait_ge(s_pt, h - 1)
                link(dve, dve.tensor_tensor(pb[h % 2], ps[4 + h % 2][:, 0:384], bias[:, h * 384:(h + 1) * 384], ALU.add))
                g.dve_steps.mark(dve.tensor_reduce(mu[:, 0:1], pb[h % 2][:, 0:P], AX.X, ALU.max))
                link(dve, dve.tensor_reduce(mu[:, 1:2], pb[h % 2][:, P:384], AX.X, ALU.max))
                dve.tensor_scalar(mx[:, 2 * h:2 * h + 2], mu[:, 0:2], -1.0, None, ALU.mult).then_inc(s_mb, 1)
            biased(0)
            biased(1)
            dve.wait_ge(s_mb, 2)
            dve.wait_ge(s_oe, TT)
            link(dve, dve.tensor_reduce(mu, o_all, AX.X, ALU.add))
            link(dve, dve.tensor_scalar(mu, mu, 1.0 / P, None, ALU.mult))
            link(dve, dve.tensor_tensor(o_all, o_all, mu.unsqueeze(2).to_broadcast([P, 8, P]), ALU.subtract))
            link(dve, dve.tensor_tensor(tmp2, tmp, tmp, ALU.mult))
            link(dve, dve.tensor_reduce(mu, tmp2.rearrange("p (g e) -> p g e", e=P), AX.X, ALU.add))
            dve.tensor_scalar(var, mu, 1.0 / P, EPS, ALU.mult, ALU.add).then_inc(s_var, 1)
            dve.wait_ge(s_std, 1)
            link(dve, dve.reciprocal(rstd, std))
            link(dve, dve.tensor_tensor(o_all, o_all, rstd.unsqueeze(2).to_broadcast([P, 8, P]), ALU.mult))
            o2 = tmp.rearrange("p (a n) -> p a n", a=TT)
            link(dve, dve.tensor_tensor(o2, o2, rgain.unsqueeze(1).to_broadcast([P, TT, HALF]), ALU.mult))
            dve.wait_ge(s_ev, 14)
            link(dve, dve.tensor_tensor(g.mixn[:, :, 0:HALF], g.mixn[:, :, 0:HALF], o2, ALU.mult))
            biased(2)
            biased(3)
            dve.wait_ge(s_ev, 16)
            dve.wait_ge(s_mo, RH)
            link(dve, dve.reciprocal(rinv, rowsum))
            for h in range(RH):
                for tt in range(TT):
                    v = g.mixn[:, tt, HALF + h * P:HALF + (h + 1) * P]
                    g.dve_steps.mark(dve.scalar_tensor_tensor(out=v, in0=ps[6 + tt][:, h * P:(h + 1) * P],
                                                              scalar=rinv[:, 2 * h + tt:2 * h + tt + 1], in1=v,
                                                              op0=ALU.mult, op1=ALU.mult))
            g.dve_steps.wait(dve)

        @block.tensor
        def _(pe):
            def project(u):
                ch, half = IN_ORDER[u // 2], u % 2
                bank = ps[unit_bank[u]]
                w = g.chunk(pe, c0 + u // 2)
                if 4 <= u < 14:
                    pe.wait_ge(s_ev, u - 3)
                if ch < 2:
                    for hh in range(2):
                        h = 2 * half + hh
                        for k in range(KT):
                            ins = pe.matmul(bank[:, hh * S:(hh + 1) * S], w[:, k, h * P:(h + 1) * P], g.hT[:, k, :],
                                            start=(k == 0), stop=(k == KT - 1))
                else:
                    for k in range(KT):
                        ins = pe.matmul(bank[:, :], g.hT[:, k, half * P:(half + 1) * P], w[:, k, :],
                                        start=(k == 0), stop=(k == KT - 1))
                ins.then_inc(s_prj, 1)

            n_pe(pe)
            n_ready(pe)
            for u in range(6):
                project(u)
            pe.wait_ge(s_ev, 4)
            for b in range(4):
                pe.matmul(bank2(ps[b]), con["rot"], raw[:, 2 * b:2 * b + 2, :], start=True, stop=True).then_inc(s_rot, 1)
            for u in range(6, 12):
                project(u)
            pe.wait_ge(s_qkn, TT)
            pe.wait_ge(s_rotd, 4)
            for b in range(4):
                for hh in range(2):
                    for tt in range(TT):
                        j = 2 * b + hh
                        ins = pe.transpose(ps[b][:, hh * S + tt * P:hh * S + tt * P + P],
                                           mqk[:, tt, j * P:(j + 1) * P], ident)
                ins.then_inc(s_qkt, 1)
            project(12)

            def ret_scores(h):
                if h >= 2:
                    pe.wait_ge(s_sT, h - 1)
                kq = rqk[:, 4 + h, :]
                pe.matmul(ps[h % 2][:, 0:S], kq[:, 0:P], rqk[:, h, :], start=True, stop=True)
                pe.matmul(ps[h % 2][:, S:384], kq[:, P:S], rqk[:, h, P:S], start=True, stop=True).then_inc(s_s, 1)

            def ret_out(h):
                pe.wait_ge(s_sT, h + 1)
                v = sT[h % 2]
                hs = slice(h * P, (h + 1) * P)
                pe.matmul(ps[6][:, hs], v[:, 0:P], rv[:, 0, hs], start=True, stop=True)
                pe.matmul(ps[7][:, hs], v[:, P:S], rv[:, 0, hs], start=True, stop=False)
                pe.matmul(ps[7][:, hs], v[:, S:384], rv[:, 1, hs], start=False, stop=True).then_inc(s_o, 1)

            pe.wait_ge(s_qkT, 4)
            ret_scores(0)
            ret_scores(1)
            project(13)
            pe.wait_ge(s_ev, 12)
            for h in range(RH):
                ret_out(h)
                if h + 2 < RH:
                    ret_scores(h + 2)

            def moba_scores(h):
                if h >= 2:
                    pe.wait_ge(s_mb, h - 1)
                pe.matmul(ps[4 + h % 2][:, 0:P], mqkT[:, h, 0:P], mqkT[:, 4 + h, 0:P], start=True, stop=True)
                pe.matmul(ps[4 + h % 2][:, P:384], mqkT[:, h, P:S], mqkT[:, 4 + h, :], start=True, stop=True).then_inc(s_ms, 1)

            pe.wait_ge(s_ev, 14)
            moba_scores(0)
            moba_scores(1)
            pe.wait_ge(s_sT, RH)
            project(14)
            project(15)
            for h in range(RH):
                pe.wait_ge(s_p, 2 * h + 2)
                if h >= 2:
                    pe.wait_ge(s_pT, h - 1)
                for j in range(3):
                    ins = pe.transpose(ps[2 + h % 2][:, j * P:(j + 1) * P], pb[h % 2][:, j * P:(j + 1) * P], ident)
                ins.then_inc(s_pt, 1)
                pe.wait_ge(s_pT, h + 1)
                if h == 0:
                    pe.wait_ge(s_oe, TT)
                hs = slice(h * P, (h + 1) * P)
                v = pbT[h % 2]
                pe.matmul(ps[6][:, hs], v[:, 0:P], mv[:, 0, hs], start=True, stop=True)
                pe.matmul(ps[7][:, hs], v[:, P:S], mv[:, 0, hs], start=True, stop=False)
                pe.matmul(ps[7][:, hs], v[:, S:384], mv[:, 1, hs], start=False, stop=True).then_inc(s_mo, 1)
                if h + 2 < RH:
                    moba_scores(h + 2)

    m_pe, m_act, m_ready = stage_mixT(g, n_ + "_out", list(range(KT)))
    n_act, n_dve, n_pe, n_ready = stage_norm(g, n_ + "_ple", None)
    s_y, s_x = g.sem(n_ + "_y"), g.sem(n_ + "_x")
    s_pt2, s_pT2 = g.sem(n_ + "_ple_in_transposed"), g.sem(n_ + "_ple_pT")
    s_e, s_ev, s_g, s_gs, s_gu = (g.sem(n_ + k) for k in ("_e", "_e_copied", "_gate", "_gate_sigmoid", "_gate_used"))
    s_em, s_er = g.sem(n_ + "_e_mean"), g.sem(n_ + "_e_root")
    for i, when in enumerate(((s_y, 2), (s_y, 4), (s_e, 4), (s_g, 2), (s_g, 4))):
        g.free_when[c0 + 8 + i] = when
    e = g.mixn
    sig = [tmp[:, 0:512], tmp[:, 512:1024]]
    with nc.Block() as block:
        @block.sync
        def _(sp):
            g.send(sp, c0 + 13 + SLOTS)

        @block.scalar
        def _(act):
            m_act(act)
            act.wait_ge(s_pt2, 1)
            act.copy(pT, bank2(ps[0])).then_inc(s_pT2, 1)
            for j in range(4):
                act.wait_ge(s_e, j + 1)
                act.copy(e[:, j // 2, (j % 2) * 512:(j % 2 + 1) * 512], ps[j][:, :]).then_inc(s_ev, 1)
            act.wait_ge(s_ev, 4)
            act.wait_ge(s_x, 4)
            n_act(act)
            for tt in range(TT):
                ins = act.activation(tmp2, e[:, tt, :], ACT.Square, accum_out=sm[:, 16 + tt:17 + tt])
                g.act_steps.link(act, ins)
            act.mul(sm[:, 18:20], sm[:, 16:18], 1.0 / D).then_inc(s_em, 1)
            act.wait_ge(s_em, 2)
            act.activation(sm[:, 22:24], sm[:, 20:22], ACT.Sqrt).then_inc(s_er, 1)
            for j in range(4):
                act.wait_ge(s_g, j + 1)
                if j >= 2:
                    act.wait_ge(s_gu, j - 1)
                act.activation(sig[j % 2], ps[4 + j][:, :], ACT.Sigmoid).then_inc(s_gs, 1)

        @block.vector
        def _(dve):
            for j in range(4):
                ch, tt = divmod(j, 2)
                v = g.x[:, tt, ch * 512:(ch + 1) * 512]
                dve.wait_ge(s_y, j + 1)
                dve.tensor_tensor(v, v, ps[4 + j][:, :], ALU.add).then_inc(s_x, 1)
            n_dve(dve)
            dve.wait_ge(s_em, 1)
            dve.tensor_scalar(sm[:, 20:22], sm[:, 18:20], EPS, None, ALU.add).then_inc(s_em, 1)
            dve.wait_ge(s_er, 1)
            g.dve_steps.link(dve, dve.reciprocal(sm[:, 24:26], sm[:, 22:24]))
            for tt in range(TT):
                g.dve_steps.mark(dve.scalar_tensor_tensor(out=e[:, tt, :], in0=e[:, tt, :], scalar=sm[:, 24 + tt:25 + tt],
                                                          in1=pgain, op0=ALU.mult, op1=ALU.mult))
            g.dve_steps.wait(dve)
            for j in range(4):
                ch, tt = divmod(j, 2)
                cols = slice(ch * 512, (ch + 1) * 512)
                dve.wait_ge(s_gs, j + 1)
                g.dve_steps.link(dve, dve.tensor_tensor(e[:, tt, cols], e[:, tt, cols], sig[j % 2], ALU.mult))
                dve.tensor_tensor(g.x[:, tt, cols], g.x[:, tt, cols], e[:, tt, cols], ALU.add).then_inc(s_gu, 1)

        @block.tensor
        def _(pe):
            m_pe(pe)
            m_ready(pe)
            for j in range(4):
                ch, tt = divmod(j, 2)
                ins = project_natural(g, pe, c0 + 8 + ch, g.mixT, ps[4 + j][:, :], tt, slice(0, 512))
                ins.then_inc(s_y, 1)
            for kk in range(2):
                for tt in range(TT):
                    ins = pe.transpose(ps[0][:, kk * S + tt * P:kk * S + tt * P + P], ptok[:, tt, kk * P:(kk + 1) * P], ident)
            ins.then_inc(s_pt2, 1)
            pe.wait_ge(s_pT2, 1)
            for j in range(4):
                ins = project_natural(g, pe, c0 + 10, pT, ps[j][:, :], j // 2, slice((j % 2) * 512, (j % 2 + 1) * 512))
                ins.then_inc(s_e, 1)
            pe.wait_ge(s_ev, 4)
            n_pe(pe)
            n_ready(pe)
            pe.wait_ge(s_x, 4)
            for j in range(4):
                ch, tt = divmod(j, 2)
                ins = project_natural(g, pe, c0 + 11 + ch, g.hT, ps[4 + j][:, :], tt, slice(0, 512))
                ins.then_inc(s_g, 1)
    g.end_phase()
    return c0 + 13


def even_layer(g, c0):
    nc, A, ps = g.nc, g.A, g.ps
    g.at = 0
    ident = g.con("ident")
    cols = g.take(64)
    gcol, mu, w0, a0 = cols[:, 0:8], cols[:, 8:22], cols[:, 22:26], cols[:, 26:30]
    k_k, k_a, r_k, pscale, one_ka = (cols[:, c:c + 4] for c in (30, 34, 38, 42, 46))
    lora = g.take(HALF)
    g2 = g.take(HALF)
    pool_w = g.take(4 * P).rearrange("p (g d) -> p g d", g=4)
    lnb = g.take(HALF)
    lng = g.take(HALF)
    n_even = sum(n for _, n in g.where_even.values())
    ec = g.take(n_even)
    con = {k: ec[:, at:at + n] for k, (at, n) in g.where_even.items()}

    def tiles(n=4):
        return g.take(n * S).rearrange("p (a t) -> p a t", a=n)

    m = tiles(14)
    r, k, v, dg = m[:, 0:4, :], m[:, 4:8, :], m[:, 8:12, :], m[:, 12:14, :]
    L, E, a, kk = tiles(), tiles(), tiles(), tiles()
    vn = g.take(TT * HALF).rearrange("p (a n) -> p a n", a=TT)
    gn = g.take(TT * HALF).rearrange("p (a n) -> p a n", a=TT)
    mixT_flat = g.mixT[:, :, :].rearrange("p k t -> p (k t)")
    ub = [mixT_flat[:, i * 514:(i + 1) * 514].rearrange("p (a t) -> p a t", a=2) for i in range(2)]
    upool = g.mixn[:, :, HALF:]
    sm = g.small
    s_par = g.sem("even_params_landed")
    s_prj, s_ev, s_sh = g.sem("even_projected"), g.sem("even_evacuated"), g.sem("even_shifted")
    s_z = g.sem("even_shift_zeros")
    s_gain = g.sem("even_gain_landed")
    n_act, n_dve, n_pe, n_ready = stage_norm(g, "even_in", gcol, s_gain)
    for c in range(3):
        g.free_when[c0 + c] = (s_prj, 2 * c + 2)
    g.free_when[c0 + 3] = (s_prj, 7)
    g.free_when[c0 + 4] = (s_prj, 9)
    lw, tmp = (g.xs[:, i, :].rearrange("p (a t) -> p a t", a=4) for i in range(2))
    xsn = g.xs
    dT = g.mixT[:, 0:4, :]
    lend = sm[:, 128:144]
    bonus = sm[:, 144:160]
    flat = lambda ap: ap.rearrange("p a t -> p (a t)")
    bc = lambda col: col.unsqueeze(2).to_broadcast([P, 4, S])
    s_th, s_zz, s_sg, s_aa = g.sem("even_tanh"), g.sem("even_z"), g.sem("even_sigmoids"), g.sem("even_a")
    s_vt, s_cp = g.sem("even_v_g_natural"), g.sem("even_v_g_copied")
    s_sq, s_ss, s_rt = g.sem("even_kk_squares"), g.sem("even_kk_sums"), g.sem("even_kk_roots")
    s_L, s_Ep, s_En, s_Ev, s_ue = (g.sem(f"even_{n}") for n in ("L", "exp_L", "exp_minus_L", "exp_prev", "exp_used"))
    s_b, s_bo = g.sem("even_bonus_in"), g.sem("even_bonus")
    s_kb, s_kt, s_kc = g.sem("even_k_b_decayed"), g.sem("even_k_b_transposed"), g.sem("even_k_b_copied")
    s_pd, s_pdc, s_py, s_pyc = g.sem("pool_diff"), g.sem("pool_diff_copied"), g.sem("pool_y"), g.sem("pool_y_copied")
    with nc.Block() as block:
        @block.sync
        def _(sp):
            sp.dma_start(gcol, A["even_norm_g"]).then_inc(s_gain, 16)
            for dst, name in ((mu, "rw_mu"), (w0, "rw_w0"), (a0, "rw_a0"), (k_k, "rw_k_k"),
                              (k_a, "rw_k_a"), (r_k, "rw_r_k"), (pscale, "pool_scale"), (ec, "c_even")):
                sp.dma_start(dst, A[name]).then_inc(s_par, 16)
            sp.dma_start(lora[0:64, :], A["rw_w2"][0]).then_inc(s_par, 16)
            sp.dma_start(lora[64:P, :], A["rw_a2"][0]).then_inc(s_par, 16)
            sp.dma_start(g2, A["rw_g2"][0]).then_inc(s_par, 16)
            sp.dma_start(pool_w, A["pool_w"][0].rearrange("g c d -> c g d")).then_inc(s_par, 16)
            sp.dma_start(lng, A["rw_ln_g"][0].partition_broadcast(P)).then_inc(s_par, 16)
            sp.dma_start(lnb, A["rw_ln_b"][0].partition_broadcast(P)).then_inc(s_par, 16)
            g.send(sp, c0 + 5 + SLOTS)

        @block.scalar
        def _(act):
            def copy_out(u):
                bank = ps[4 + u % 4]
                act.wait_ge(s_prj, u + 1)
                if u < 7:
                    if u >= 2:
                        act.wait_ge(s_sh, u - 1)
                    ins = act.copy(ub[u % 2][:, :, 1:257], bank2(bank))
                else:
                    ins = act.copy(upool[:, u - 7, :], bank[:, :])
                ins.then_inc(s_ev, 1)

            n_act(act)
            act.wait_ge(s_z, 2)
            for u in range(7):
                copy_out(u)
            act.wait_ge(s_sh, 7)
            act.activation(dg[0:64, 0, :], dg[0:64, 0, :], ACT.Tanh).then_inc(s_th, 1)
            act.activation(dg[:, 1, :], dg[:, 1, :], ACT.Sigmoid).then_inc(s_th, 1)
            copy_out(7)
            act.wait_ge(s_zz, 1)
            for n in range(4):
                act.activation(lw[:, n, :], ps[n // 2][:, (n % 2) * S:(n % 2 + 1) * S], ACT.Sigmoid,
                               bias=w0[:, n:n + 1]).then_inc(s_sg, 1)
            act.wait_ge(s_zz, 2)
            for n in range(4):
                act.activation(a[:, n, :], ps[2 + n // 2][:, (n % 2) * S:(n % 2 + 1) * S], ACT.Sigmoid,
                               bias=a0[:, n:n + 1]).then_inc(s_aa, 1)
            copy_out(8)
            act.wait_ge(s_vt, 2)
            for tt in range(TT):
                act.copy(gn[:, tt, :], ps[4 + tt][:, :]).then_inc(s_cp, 1)
                act.copy(vn[:, tt, :], ps[6 + tt][:, :]).then_inc(s_cp, 1)
            act.wait_ge(s_ss, 2)
            for i in range(2):
                act.activation(tmp[:, 2 * i:2 * i + 2, :], bank2(ps[i]), ACT.Sqrt).then_inc(s_rt, 1)
            act.wait_ge(s_L, 1)
            act.activation(lend.rearrange("p (a c) -> p a c", a=4), L[:, :, CH - 1::CH], ACT.Exp).then_inc(s_Ep, 1)
            act.activation(E, L, ACT.Exp).then_inc(s_Ep, 1)
            act.wait_ge(s_ue, 1)
            act.activation(E, lw, ACT.Exp).then_inc(s_Ev, 1)
            act.wait_ge(s_ue, 2)
            act.activation(E, L, ACT.Exp, scale=-1.0).then_inc(s_En, 1)
            for q in range(2):
                act.wait_ge(s_pd, q + 1)
                act.copy(dT[:, 2 * q:2 * q + 2, :], bank2(ps[4 + q])).then_inc(s_pdc, 1)
            for q in range(4):
                act.wait_ge(s_py, q // 2 + 1)
                act.activation(g.mixT[:, 4 + q, :], ps[6 + q // 2][:, (q % 2) * S:(q % 2 + 1) * S], ACT.Copy,
                               scale=pscale[:, q:q + 1]).then_inc(s_pyc, 1)
            for b in range(4):
                act.wait_ge(s_kt, b + 1)
                tt = b % 2
                act.copy(xsn[:, tt, (b // 2) * HALF:(b // 2 + 1) * HALF], ps[b][:, :]).then_inc(s_kc, 1)
            act.wait_ge(s_bo, 1)
            g.act_steps.link(act, act.copy(bonus, ps[4][:, 0:16]))

        @block.vector
        def _(dve):
            for i in range(2):
                dve.memset(ub[i][:, :, 0:1], 0.0).then_inc(s_z, 1)
            n_dve(dve)
            dve.wait_ge(s_par, 16 * 14)
            for u in range(7):
                dve.wait_ge(s_ev, u + 1)
                if u:
                    dve.wait_ge(s_sh, u)
                dif = E[:, 0:2, :]
                g.dve_steps.link(dve, dve.tensor_tensor(dif, ub[u % 2][:, :, 0:S], ub[u % 2][:, :, 1:257], ALU.subtract))
                for i in range(2):
                    ins = dve.scalar_tensor_tensor(out=m[:, 2 * u + i, :], in0=dif[:, i, :],
                                                   scalar=mu[:, 2 * u + i:2 * u + i + 1], in1=ub[u % 2][:, i, 1:257],
                                                   op0=ALU.mult, op1=ALU.add)
                    if i == 0:
                        g.dve_steps.mark(ins)
                    else:
                        ins.then_inc(s_sh, 1)
            dve.wait_ge(s_sh, 7)
            g.dve_steps.wait(dve)
            link = g.dve_steps.link
            link(dve, dve.tensor_tensor(kk, k, bc(k_k), ALU.mult))
            dve.tensor_tensor(tmp, kk, kk, ALU.mult).then_inc(s_sq, 1)
            link(dve, dve.tensor_scalar(one_ka, k_a, -1.0, 1.0, ALU.mult, ALU.add))
            dve.wait_ge(s_sg, 4)
            link(dve, dve.tensor_scalar(lw, lw, -float(np.exp(-0.5)), None, ALU.mult))
            for n in range(4):
                g.dve_steps.mark(dve.tensor_tensor_scan(L[:, n, :], con["reset"], lw[:, n, :], 0.0, ALU.mult, ALU.add))
            g.dve_steps.wait(dve)
            dve.tensor_tensor(lw, L, lw, ALU.subtract).then_inc(s_L, 1)
            dve.wait_ge(s_rt, 2)
            link(dve, dve.tensor_scalar(tmp, tmp, 1e-12, None, ALU.max))
            link(dve, dve.reciprocal(tmp, tmp))
            link(dve, dve.tensor_tensor(kk, kk, tmp, ALU.mult))
            dve.wait_ge(s_aa, 4)
            link(dve, dve.tensor_tensor(tmp, a, bc(k_a), ALU.mult))
            link(dve, dve.tensor_tensor(tmp, tmp, bc(one_ka), ALU.add))
            link(dve, dve.tensor_tensor(k, k, tmp, ALU.mult))
            link(dve, dve.tensor_tensor(tmp, r, k, ALU.mult))
            dve.tensor_tensor(tmp, tmp, bc(r_k), ALU.mult).then_inc(s_b, 1)
            link(dve, dve.tensor_tensor(a, a, kk, ALU.mult))
            dve.wait_ge(s_Ep, 2)
            dve.tensor_tensor(r, r, E, ALU.mult).then_inc(s_ue, 1)
            dve.wait_ge(s_Ev, 1)
            dve.scalar_tensor_tensor(out=flat(kk), in0=flat(kk), scalar=-1.0, in1=flat(E), op0=ALU.mult, op1=ALU.mult)\
               .then_inc(s_ue, 1)
            dve.wait_ge(s_En, 1)
            dve.tensor_tensor(k, k, E, ALU.mult).then_inc(s_kb, 1)
            dve.tensor_tensor(a, a, E, ALU.mult).then_inc(s_kb, 1)
            dve.wait_ge(s_kb, 2)

        @block.tensor
        def _(pe):
            def project(u):
                bank = ps[4 + u % 4]
                ch = u // 2 if u < 6 else (3 if u == 6 else 4)
                w = g.chunk(pe, c0 + ch)
                if u >= 4:
                    pe.wait_ge(s_ev, u - 3)
                if u < 7:
                    for i in range(2):
                        n = (2 * (u % 2) + i if u < 6 else i) * P
                        for kt in range(KT):
                            ins = pe.matmul(bank[:, i * S:(i + 1) * S], w[:, kt, n:n + P], g.hT[:, kt, :],
                                            start=(kt == 0), stop=(kt == KT - 1))
                else:
                    ins = project_natural(g, pe, c0 + ch, g.hT, bank[:, :], u - 7, slice(0, 512))
                ins.then_inc(s_prj, 1)

            n_pe(pe)
            n_ready(pe)
            for u in range(8):
                project(u)
            pe.wait_ge(s_th, 2)
            for n in range(4):
                ins = pe.matmul(ps[n // 2][:, (n % 2) * S:(n % 2 + 1) * S], lora[0:64, n * P:(n + 1) * P], dg[0:64, 0, :],
                                start=True, stop=True)
            ins.then_inc(s_zz, 1)
            for n in range(4):
                ins = pe.matmul(ps[2 + n // 2][:, (n % 2) * S:(n % 2 + 1) * S], lora[64:P, n * P:(n + 1) * P],
                                dg[64:P, 0, :], start=True, stop=True)
            ins.then_inc(s_zz, 1)
            project(8)
            pe.wait_ge(s_ev, 8)
            for tt in range(TT):
                for n in range(4):
                    pe.transpose(ps[6 + tt][:, n * P:(n + 1) * P], v[:, n, tt * P:(tt + 1) * P], ident)
            pe.wait_ge(s_ev, 9)
            for tt in range(TT):
                pe.matmul(ps[4 + tt][:, :], dg[:, 1, tt * P:(tt + 1) * P], g2, start=True, stop=True).then_inc(s_vt, 1)
            pe.wait_ge(s_sq, 1)
            pe.wait_ge(s_sg, 4)
            for i in range(2):
                pe.matmul(bank2(ps[i]), g.con("head64"), tmp[:, 2 * i:2 * i + 2, :], start=True, stop=True).then_inc(s_ss, 1)
            pe.wait_ge(s_cp, 4)
            pm = con["pool"].rearrange("p (a g t) -> p a g t", a=TT, g=4)
            for q in range(4):
                for st in range(TT):
                    ins = pe.matmul(ps[4 + q // 2][:, (q % 2) * S:(q % 2 + 1) * S], upool[:, st, q * P:(q + 1) * P],
                                    pm[:, st, q, :], start=(st == 0), stop=(st == 1))
                if q % 2:
                    ins.then_inc(s_pd, 1)
            for q in range(4):
                pe.wait_ge(s_pdc, q // 2 + 1)
                ins = pe.matmul(ps[6 + q // 2][:, (q % 2) * S:(q % 2 + 1) * S], pool_w[:, q, :], dT[:, q, :],
                                start=True, stop=True)
                if q % 2:
                    ins.then_inc(s_py, 1)
            pe.wait_ge(s_b, 1)
            for tt in range(TT):
                for n in range(4):
                    c = tt * 8 + 2 * n
                    ins = pe.matmul(ps[4][:, c:c + 2], tmp[:, n, tt * P:(tt + 1) * P], g.con("head64")[:, 0:P:64],
                                    start=True, stop=True)
            ins.then_inc(s_bo, 1)
            for b in range(4):
                src = (k, a)[b // 2]
                tt = b % 2
                pe.wait_ge(s_kb, b // 2 + 1)
                pe.wait_ge(s_rt, 2)
                pe.wait_ge(s_aa, 4)
                for n in range(4):
                    ins = pe.transpose(ps[b][:, n * P:(n + 1) * P], src[:, n, tt * P:(tt + 1) * P], ident)
                ins.then_inc(s_kt, 1)

    at0 = g.where_even["pool"][0]
    spare = ec[:, at0:at0 + 2048]
    place = lambda h: 4 * (h % 2) + h // 2
    Aab = spare[:, 0:1024].rearrange("p (h t) -> p h t", h=8)
    off = spare[:, 1024:2048].rearrange("p (h t) -> p h t", h=8)
    T = flat(v).rearrange("p (h t) -> p h t", h=8)
    Z = flat(dT).rearrange("p (h t) -> p h t", h=8)
    Aak, Ark = T, Z
    TTr = g.hT[:, :, :].rearrange("p k t -> p (k t)").rearrange("p (a h t) -> p a h t", a=TT, h=8)
    Arb = g.mixn[:, :, :].rearrange("p a (h t) -> p a h t", h=8)
    AkV = flat(L).rearrange("p (a n) -> p a n", a=TT)
    y0 = flat(E).rearrange("p (a n) -> p a n", a=TT)
    s_A, s_M, s_AV, s_AVc = g.sem("rwkv_A"), g.sem("rwkv_A_masked"), g.sem("rwkv_AV"), g.sem("rwkv_AV_copied")
    s_T0, s_T0c, s_off = g.sem("rwkv_T_transposed"), g.sem("rwkv_T_copied"), g.sem("rwkv_off")
    s_Z, s_Zc, s_dT, s_up = g.sem("rwkv_Z"), g.sem("rwkv_Z_copied"), g.sem("rwkv_dT"), g.sem("rwkv_T_updated")
    four = lambda ap, q: ap[:, 4 * q:4 * q + 4, :]
    b4 = lambda bank: bank[:, :].rearrange("p (h t) -> p h t", h=4)
    mask4 = lambda mk: mk.unsqueeze(1).to_broadcast([P, 4, P])
    with nc.Block() as block:
        @block.scalar
        def _(act):
            for tt in range(TT):
                for q in range(2):
                    act.wait_ge(s_AV, 2 * tt + q + 1)
                    act.copy((AkV, y0)[q][:, tt, :], ps[q][:, :]).then_inc(s_AVc, 1)
                for q in range(2):
                    act.wait_ge(s_T0, 2 * tt + q + 1)
                    act.copy(four(T, q), b4(ps[2 + q])).then_inc(s_T0c, 1)
                for lev in range(1, 6):
                    for q in range(2):
                        act.wait_ge(s_Z, 10 * tt + 2 * (lev - 1) + q + 1)
                        act.copy(four(Z, q), b4(ps[q])).then_inc(s_Zc, 1)

        @block.vector
        def _(dve):
            link = g.dve_steps.link
            for tt in range(TT):
                for j in range(8):
                    q = j % 2
                    dst = (four(Aab, q), four(Aak, q), four(Arb[:, tt], q), four(Ark, q))[j // 2]
                    dve.wait_ge(s_A, 8 * tt + j + 1)
                    if tt == 1 and j == 0:
                        dve.wait_ge(s_Z, 10)
                        dve.wait_ge(s_dT, 18)
                    dve.tensor_tensor(dst, b4(ps[j]), mask4(g.con("lt" if j < 4 else "le")), ALU.mult).then_inc(s_M, 1)
                dve.wait_ge(s_M, 8 * tt + 8)
                for q in range(2):
                    link(dve, dve.tensor_tensor(four(TTr[:, tt], q), four(Aab, q), mask4(con["lev0"]), ALU.mult))
                    dve.tensor_tensor(four(TTr[:, tt], q), four(TTr[:, tt], q), mask4(ident), ALU.add).then_inc(s_off, 1)
                for lev in range(1, 6):
                    for q in range(2):
                        if lev > 1:
                            dve.wait_ge(s_Z, 10 * tt + 2 * (lev - 2) + q + 1)
                        dve.tensor_tensor(four(off, q), four(Aab, q), mask4(con[f"lev{lev}"]), ALU.mult).then_inc(s_off, 1)
                    for q in range(2):
                        dve.wait_ge(s_dT, 18 * tt + (4 * (lev - 1) + 2 * q + 2 if lev < 5 else 16 + q + 1))
                        dve.wait_ge(s_T0c, 2 * tt + q + 1)
                        if lev < 5:
                            link(dve, dve.tensor_tensor(four(T, q), four(T, q), b4(ps[4 + 2 * q]), ALU.add))
                        dve.tensor_tensor(four(TTr[:, tt], q), four(TTr[:, tt], q), b4(ps[5 + 2 * q]), ALU.add)\
                           .then_inc(s_up, 1)
                dve.wait_ge(s_up, 10 * tt + 10)

        @block.tensor
        def _(pe):
            for tt in range(TT):
                tk = slice(tt * P, (tt + 1) * P)
                for j in range(8):
                    left, right = ((a, kk), (k, kk), (a, r), (k, r))[j // 2]
                    if tt == 1:
                        pe.wait_ge(s_up, 10)
                        pe.wait_ge(s_Zc, 10)
                    for i in range(4):
                        h = 2 * i + j % 2
                        q0 = 64 * (h % 2)
                        ins = pe.matmul(ps[j][:, i * P:(i + 1) * P], left[q0:q0 + 64, h // 2, tk],
                                        right[q0:q0 + 64, h // 2, tk], start=True, stop=True)
                    ins.then_inc(s_A, 1)
                pe.wait_ge(s_M, 8 * tt + 8)
                for q in range(2):
                    for h in range(8):
                        ins = pe.matmul(ps[q][:, h * 64:(h + 1) * 64], (Aak, Ark)[q][:, place(h), :],
                                        vn[:, tt, h * 64:(h + 1) * 64], start=True, stop=True)
                    ins.then_inc(s_AV, 1)
                for q in range(2):
                    pe.wait_ge(s_off, 12 * tt + q + 1)
                    for i in range(4):
                        ins = pe.transpose(ps[2 + q][:, i * P:(i + 1) * P], TTr[:, tt, 4 * q + i, :], ident)
                    ins.then_inc(s_T0, 1)
                pe.wait_ge(s_AVc, 2 * tt + 2)
                for lev in range(1, 6):
                    for q in range(2):
                        pe.wait_ge(s_off, 12 * tt + 2 * lev + q + 1)
                        pe.wait_ge(s_T0c, 2 * tt + q + 1)
                        if lev > 1:
                            pe.wait_ge(s_up, 10 * tt + 2 * (lev - 2) + q + 1)
                            pe.wait_ge(s_Zc, 10 * tt + 2 * (lev - 2) + q + 1)
                        for i in range(4):
                            ins = pe.matmul(ps[q][:, i * P:(i + 1) * P], off[:, 4 * q + i, :], T[:, 4 * q + i, :],
                                            start=True, stop=True)
                        ins.then_inc(s_Z, 1)
                    for q in range(2):
                        pe.wait_ge(s_Zc, 10 * tt + 2 * (lev - 1) + q + 1)
                        if lev < 5:
                            for i in range(4):
                                ins = pe.matmul(ps[4 + 2 * q][:, i * P:(i + 1) * P], TTr[:, tt, 4 * q + i, :],
                                                Z[:, 4 * q + i, :], start=True, stop=True)
                            ins.then_inc(s_dT, 1)
                        for i in range(4):
                            ins = pe.matmul(ps[5 + 2 * q][:, i * P:(i + 1) * P], Z[:, 4 * q + i, :],
                                            TTr[:, tt, 4 * q + i, :], start=True, stop=True)
                        ins.then_inc(s_dT, 1)

    St = [spare[:, i * 256:(i + 1) * 256].rearrange("p (a i) -> p a i", a=4) for i in range(2)]
    Ssum = spare[:, 512:768].rearrange("p (a i) -> p a i", a=4)
    X = spare[:, 768:1280]
    U = flat(dT).rearrange("p (a n) -> p a n", a=TT)
    y, ysq = flat(v), spare[:, 1024:2048]
    byp = lambda ap: ap.rearrange("p (a q i) -> p a q i", q=2, i=64)
    b64 = lambda bank: bank[:, :].rearrange("p (h i) -> p h i", i=64)
    s_S, s_X, s_Xc, s_U, s_Uc, s_dS, s_y, s_ye = (g.sem("rwkv_" + n) for n in (
        "state", "X", "X_copied", "U", "U_copied", "dS", "y", "y_copied"))
    s_var, s_std, s_mix = g.sem("rwkv_var"), g.sem("rwkv_std"), g.sem("rwkv_mixed")
    mu_, var, std, rstd = sm[:, 160:176], sm[:, 176:192], sm[:, 192:208], sm[:, 208:224]
    with nc.Block() as block:
        @block.scalar
        def _(act):
            for c in range(4):
                q0 = 64 * (c % 2)
                act.wait_ge(s_U, c + 1)
                act.copy(U[q0:q0 + 64, c // 2, :], ps[2][q0:q0 + 64, :]).then_inc(s_Uc, 1)
            act.wait_ge(s_var, 1)
            act.activation(std, var, ACT.Sqrt).then_inc(s_std, 1)

        @block.vector
        def _(dve):
            link = g.dve_steps.link
            dve.memset(St[0], 0.0).then_inc(s_S, 1)
            for c in range(4):
                q0 = 64 * (c % 2)
                dve.wait_ge(s_X, c + 1)
                if c:
                    dve.wait_ge(s_U, c)
                for q in range(2):
                    dve.tensor_tensor(byp(X)[q0:q0 + 64, :, q, :], b64(ps[q])[q0:q0 + 64, 0:4, :],
                                      byp(AkV[:, c // 2, :])[q0:q0 + 64, :, q, :], ALU.add).then_inc(s_Xc, 1)
                if c == 3:
                    break
                dve.wait_ge(s_dS, c + 1)
                if c >= 1:
                    dve.wait_ge(s_y, c)
                link(dve, dve.tensor_tensor(Ssum, ps[3][:, 0:256].rearrange("p (a i) -> p a i", a=4), St[c % 2], ALU.add))
                dec = lend.rearrange("p (a c) -> p a c", a=4)[:, :, c:c + 1].to_broadcast([P, 4, 64])
                dve.tensor_tensor(St[(c + 1) % 2], Ssum, dec, ALU.mult).then_inc(s_S, 1)
                dve.wait_ge(s_S, c + 2)
            y2 = y.rearrange("p (a n) -> p a n", a=TT)
            yh = y.rearrange("p (g e) -> p g e", e=64)
            b16 = lambda col: col.unsqueeze(2).to_broadcast([P, 16, 64])
            dve.wait_ge(s_y, 4)
            for tt in range(TT):
                g.dve_steps.mark(dve.tensor_tensor(y2[:, tt, :], ps[6 + tt][:, :], y0[:, tt, :], ALU.add))
            g.dve_steps.wait(dve)
            for tt in range(TT):
                for q in range(2):
                    yv = byp(y2[:, tt, :])[:, :, q, :]
                    g.dve_steps.mark(dve.tensor_tensor(yv, yv, b64(ps[4 + q])[:, 4 * tt:4 * tt + 4, :], ALU.add))
            g.dve_steps.wait(dve)
            link(dve, dve.tensor_reduce(mu_, yh, AX.X, ALU.add))
            link(dve, dve.tensor_scalar(mu_, mu_, 1.0 / 64, None, ALU.mult))
            link(dve, dve.tensor_tensor(yh, yh, b16(mu_), ALU.subtract))
            link(dve, dve.tensor_tensor(ysq, y, y, ALU.mult))
            link(dve, dve.tensor_reduce(mu_, ysq.rearrange("p (g e) -> p g e", e=64), AX.X, ALU.add))
            dve.tensor_scalar(var, mu_, 1.0 / 64, LN_EPS, ALU.mult, ALU.add).then_inc(s_var, 1)
            dve.wait_ge(s_std, 1)
            link(dve, dve.reciprocal(rstd, std))
            link(dve, dve.tensor_tensor(yh, yh, b16(rstd), ALU.mult))
            row = lambda w: w.unsqueeze(1).to_broadcast([P, TT, HALF])
            link(dve, dve.tensor_tensor(y2, y2, row(lng), ALU.mult))
            link(dve, dve.tensor_tensor(y2, y2, row(lnb), ALU.add))
            vh = flat(vn).rearrange("p (g e) -> p g e", e=64)
            link(dve, dve.tensor_tensor(vh, vh, b16(bonus), ALU.mult))
            link(dve, dve.tensor_tensor(y2, y2, vn, ALU.add))
            link(dve, dve.tensor_tensor(g.mixn[:, :, 0:HALF], y2, gn, ALU.mult))

        @block.tensor
        def _(pe):
            def outputs(c):
                q0, tt = 64 * (c % 2), c // 2
                tk = slice(c * CH, (c + 1) * CH)
                for h in range(8):
                    p0 = 64 * (h % 2)
                    col = (4 * tt + h // 2) * 64
                    pe.matmul(ps[4 + h % 2][q0:q0 + 64, col:col + 64], r[p0:p0 + 64, h // 2, tk],
                              St[c % 2][p0:p0 + 64, h // 2, :], start=True, stop=True)
                for h in range(8):
                    ins = pe.matmul(ps[6 + tt][q0:q0 + 64, h * 64:(h + 1) * 64], Arb[q0:q0 + 64, tt, place(h), q0:q0 + 64],
                                    U[q0:q0 + 64, tt, h * 64:(h + 1) * 64], start=True, stop=True)
                ins.then_inc(s_y, 1)

            for c in range(4):
                q0, tt = 64 * (c % 2), c // 2
                tk = slice(c * CH, (c + 1) * CH)
                pe.wait_ge(s_S, c + 1)
                if c:
                    pe.wait_ge(s_Xc, 2 * c)
                for h in range(8):
                    p0 = 64 * (h % 2)
                    ins = pe.matmul(ps[h % 2][q0:q0 + 64, (h // 2) * 64:(h // 2 + 1) * 64], kk[p0:p0 + 64, h // 2, tk],
                                    St[c % 2][p0:p0 + 64, h // 2, :], start=True, stop=True)
                ins.then_inc(s_X, 1)
                if c:
                    outputs(c - 1)
                pe.wait_ge(s_Xc, 2 * c + 2)
                if c:
                    pe.wait_ge(s_Uc, c)
                for h in range(8):
                    ins = pe.matmul(ps[2][q0:q0 + 64, h * 64:(h + 1) * 64], TTr[q0:q0 + 64, tt, place(h), q0:q0 + 64],
                                    X[q0:q0 + 64, h * 64:(h + 1) * 64], start=True, stop=True)
                ins.then_inc(s_U, 1)
                pe.wait_ge(s_Uc, c + 1)
                if c == 3:
                    break
                for h in range(8):
                    p0 = 64 * (h % 2)
                    o = ps[3][p0:p0 + 64, (h // 2) * 64:(h // 2 + 1) * 64]
                    hs = slice(h * 64, (h + 1) * 64)
                    pe.matmul(o, xsn[q0:q0 + 64, tt, HALF + h * 64:HALF + (h + 1) * 64], U[q0:q0 + 64, tt, hs],
                              start=True, stop=False)
                    ins = pe.matmul(o, xsn[q0:q0 + 64, tt, hs], vn[q0:q0 + 64, tt, hs], start=False, stop=True)
                ins.then_inc(s_dS, 1)
            outputs(3)

    output_projection(g, "even", c0 + 5, [0, 1, 2, 3], 0)
    g.end_phase()
    return c0 + 7


def output_projection(g, name, c0, natural, ly):
    nc, ps = g.nc, g.ps
    m_pe, m_act, m_ready = stage_mixT(g, name + "_out", natural)
    s_y, s_x = g.sem(name + "_out_y"), g.sem(name + "_out_x")
    for ch in range(2):
        g.free_when[c0 + ch] = (s_y, 2 * ch + 2)
    with nc.Block() as block:
        @block.sync
        def _(sp):
            g.send(sp, c0 + 2)
            moe_prefetch(g, sp, ly, c0 + 2)

        @block.scalar
        def _(act):
            m_act(act)

        @block.vector
        def _(dve):
            for j in range(4):
                ch, tt = divmod(j, 2)
                v = g.x[:, tt, ch * 512:(ch + 1) * 512]
                dve.wait_ge(s_y, j + 1)
                dve.tensor_tensor(v, v, ps[4 + j][:, :], ALU.add).then_inc(s_x, 1)

        @block.tensor
        def _(pe):
            m_pe(pe)
            m_ready(pe)
            for j in range(4):
                ch, tt = divmod(j, 2)
                project_natural(g, pe, c0 + ch, g.mixT, ps[4 + j][:, :], tt, slice(0, 512)).then_inc(s_y, 1)


def odd_layer(g, c0):
    nc, A, ps = g.nc, g.A, g.ps
    g.at = 0
    ident = g.con("ident")
    DH = 64
    NM = 2 * HT
    lam_init = 0.8 - 0.6 * float(np.exp(-0.3))
    scale = DH ** -0.5
    con = {}
    for k, (at, n) in g.where_odd.items():
        con[k] = g.take(n)
    gcol, dcol = g.take(KT), g.take(HT)
    qkg = g.take(2 * DH)
    subln = g.take(P)
    lams = g.take(4 * DH)
    a_re, a_im, lstep = g.take(NPAIR), g.take(NPAIR), g.take(NPAIR)
    bt = g.take(2 * HALF).rearrange("p (r a s) -> p r a s", r=2, a=HT)
    ct = g.take(2 * HALF).rearrange("p (r q c) -> p r q c", r=2, q=NPAIR)
    vn = g.take(TT * HALF).rearrange("p (a n) -> p a n", a=TT)
    uT = g.take(HT * S).rearrange("p (a t) -> p a t", a=HT)
    work = g.take(8192)
    qk = g.xs
    sm = g.small
    s_par, s_prj, s_ev = g.sem("odd_params_landed"), g.sem("odd_projected"), g.sem("odd_evacuated")
    s_gain = g.sem("odd_gain_landed")
    n_act, n_dve, n_pe, n_ready = stage_norm(g, "odd_in", gcol, s_gain)
    for c in range(4):
        g.free_when[c0 + c] = (s_prj, 2 * c + 2)
    flat3 = lambda ap: ap.rearrange("p a n -> p (a n)")
    xc = g.mixn
    xsn = work[:, 0:2048].rearrange("p (a n) -> p a n", a=TT)
    qkT = g.hT
    W3 = 3 * P
    pb = [work[:, 2048 + i * 2 * W3:2048 + (i + 1) * 2 * W3].rearrange("p (m n) -> p m n", m=2) for i in range(2)]
    attn = [work[:, 3584 + i * W3:3584 + (i + 1) * W3] for i in range(2)]
    attnT = [work[:, 4352 + i * W3:4352 + (i + 1) * W3] for i in range(2)]
    osb = work[:, 5120:6144]
    osq = work[:, 6144:7168]
    ss, msq, root, rstd = (sm[:, 160 + 32 * i:192 + 32 * i] for i in range(4))
    mx, rowsum, cf = (sm[:, 288 + 16 * i:304 + 16 * i] for i in range(3))
    pmax = sm[:, 336:340]
    lam = sm[:, 340:348]
    oss, omean, oroot, orstd = (sm[:, 352 + 8 * i:360 + 8 * i] for i in range(4))
    s_lm, s_le = g.sem("lambda_sums"), g.sem("lambda_exps")
    s_ms, s_rt = g.sem("qk_mean"), g.sem("qk_root")
    s_qk, s_qt, s_qT = g.sem("qk_rotated"), g.sem("qk_transposed"), g.sem("qkT")
    s_sc, s_mk, s_p, s_at = g.sem("da_scores"), g.sem("da_masked"), g.sem("da_p"), g.sem("da_attn")
    s_tr, s_trc, s_o, s_oe = g.sem("da_attn_transposed"), g.sem("da_attnT"), g.sem("da_out"), g.sem("da_out_copied")
    s_om, s_or = g.sem("da_out_mean"), g.sem("da_out_root")
    segs = (slice(0, P), slice(P, W3))
    with nc.Block() as block:
        @block.sync
        def _(sp):
            sp.dma_start(gcol, A["odd_norm_g"]).then_inc(s_gain, 16)
            for k, (at, n) in g.where_odd.items():
                sp.dma_start(con[k], A["c_odd"][:, at:at + n]).then_inc(s_par, 16)
            for dst, name in ((dcol, "s5_d"), (a_re, "s5_a_re"), (a_im, "s5_a_im"),
                              (lstep, "s5_log_step"), (bt, "s5_b"), (ct, "s5_c")):
                sp.dma_start(dst, A[name]).then_inc(s_par, 16)
            sp.dma_start(qkg[:, 0:DH], A["da_q_norm"][0].partition_broadcast(P)).then_inc(s_par, 16)
            sp.dma_start(qkg[:, DH:], A["da_k_norm"][0].partition_broadcast(P)).then_inc(s_par, 16)
            sp.dma_start(subln, A["da_subln"][0].partition_broadcast(P)).then_inc(s_par, 16)
            for i, name in enumerate(("da_lam_q1", "da_lam_q2", "da_lam_k1", "da_lam_k2")):
                sp.dma_start(lams[:, i * DH:(i + 1) * DH], A[name][0].partition_broadcast(P)).then_inc(s_par, 16)
            g.send(sp, c0 + 4 + SLOTS)

        @block.scalar
        def _(act):
            def copy_out(j):
                ch, half = divmod(j, 2)
                bank = ps[4 + j % 4]
                act.wait_ge(s_prj, j + 1)
                if ch < 2:
                    ins = act.copy(qk[:, half, ch * HALF:(ch + 1) * HALF], bank[:, :])
                elif ch == 2:
                    ins = act.copy(vn[:, half, :], bank[:, :])
                else:
                    ins = act.copy(uT[:, 2 * half:2 * half + 2, :], bank2(bank))
                ins.then_inc(s_ev, 1)

            n_act(act)
            for j in range(4):
                copy_out(j)
            act.wait_ge(s_lm, 1)
            act.activation(lam[:, 2:4], lam[:, 0:2], ACT.Exp).then_inc(s_le, 1)
            act.wait_ge(s_ms, 1)
            act.activation(root, msq, ACT.Sqrt).then_inc(s_rt, 1)
            for j in range(4, 8):
                copy_out(j)
            for b in range(4):
                act.wait_ge(s_qt, b + 1)
                act.copy(qkT[:, 2 * b:2 * b + 2, :], bank2(ps[4 + b])).then_inc(s_qT, 1)

            def exps(h):
                act.wait_ge(s_mk, h + 1)
                for m in range(2):
                    for tt in range(TT):
                        j = 4 * h + 2 * m + tt
                        act.activation(pb[h % 2][:, m, segs[tt]], pb[h % 2][:, m, segs[tt]], ACT.Exp, bias=mx[:, j:j + 1],
                                       scale=scale, accum_out=rowsum[:, j:j + 1]).then_inc(s_p, 1)

            exps(0)
            for h in range(HT):
                if h + 1 < HT:
                    exps(h + 1)
                act.wait_ge(s_tr, h + 1)
                act.copy(attnT[h % 2], ps[4 + h % 2][:, 0:W3]).then_inc(s_trc, 1)
            act.wait_ge(s_o, HT)
            for tt in range(TT):
                act.copy(osb[:, tt * HALF:(tt + 1) * HALF], ps[6 + tt][:, :]).then_inc(s_oe, 1)
            act.wait_ge(s_om, 1)
            act.activation(oroot, omean, ACT.Sqrt).then_inc(s_or, 1)

        @block.vector
        def _(dve):
            link = g.dve_steps.link
            n_dve(dve)
            dve.wait_ge(s_par, 16 * (len(con) + 13))
            lv = lams.rearrange("p (a n) -> p a n", a=4)
            link(dve, dve.tensor_tensor(lv[:, 0:2, :], lv[:, 0:2, :], lv[:, 2:4, :], ALU.mult))
            dve.tensor_reduce(lam[:, 0:2], lv[:, 0:2, :], AX.X, ALU.add).then_inc(s_lm, 1)
            dve.wait_ge(s_ev, 4)
            for tt in range(TT):
                link(dve, dve.tensor_tensor(xc[:, tt, :], qk[:, tt, :], qk[:, tt, :], ALU.mult))
                link(dve, dve.tensor_reduce(ss[:, 16 * tt:16 * tt + 16], xc[:, tt, :].rearrange("p (g e) -> p g e", e=DH),
                                            AX.X, ALU.add))
            dve.tensor_scalar(msq, ss, 1.0 / DH, EPS, ALU.mult, ALU.add).then_inc(s_ms, 1)
            dve.wait_ge(s_le, 1)
            link(dve, dve.tensor_tensor(lam[:, 4:5], lam[:, 3:4], lam[:, 2:3], ALU.subtract))
            link(dve, dve.tensor_scalar(lam[:, 5:6], lam[:, 4:5], -lam_init, None, ALU.add))
            dve.wait_ge(s_rt, 1)
            link(dve, dve.reciprocal(rstd, root))
            for tt in range(TT):
                v = qk[:, tt, :].rearrange("p (g e) -> p g e", e=DH)
                link(dve, dve.tensor_tensor(v, v, rstd[:, 16 * tt:16 * tt + 16].unsqueeze(2).to_broadcast([P, 2 * NM, DH]),
                                            ALU.mult))
                for i in range(2):
                    w = v[:, NM * i:NM * i + NM, :]
                    g.dve_steps.mark(dve.tensor_tensor(w, w, qkg[:, DH * i:DH * i + DH].unsqueeze(1).to_broadcast([P, NM, DH]),
                                                       ALU.mult))
                g.dve_steps.wait(dve)
                cs = [con[n][:, 32 * tt:32 * tt + 32].unsqueeze(1).to_broadcast([P, 4 * NM, 32]) for n in ("cos", "sin")]
                vh = qk[:, tt, :].rearrange("p (g e) -> p g e", e=32)
                g.dve_steps.mark(dve.tensor_tensor(xc[:, tt, :].rearrange("p (g e) -> p g e", e=32), vh, cs[0], ALU.mult))
                link(dve, dve.tensor_tensor(xsn[:, tt, :].rearrange("p (g e) -> p g e", e=32), vh, cs[1], ALU.mult))
                halves = lambda ap: ap.rearrange("p (g x e) -> p g x e", x=2, e=32)
                dst, c_, s_ = halves(qk[:, tt, :]), halves(xc[:, tt, :]), halves(xsn[:, tt, :])
                dve.tensor_tensor(dst[:, :, 0, :], c_[:, :, 0, :], s_[:, :, 1, :], ALU.subtract).then_inc(s_qk, 1)
                dve.tensor_tensor(dst[:, :, 1, :], c_[:, :, 1, :], s_[:, :, 0, :], ALU.add).then_inc(s_qk, 1)

            def masked(h):
                dve.wait_ge(s_sc, h + 1)
                if h >= 2:
                    dve.wait_ge(s_at, h - 1)
                for m in range(2):
                    g.dve_steps.mark(dve.tensor_tensor(pb[h % 2][:, m, :], ps[2 * (h % 2) + m][:, 0:W3], con["causal"], ALU.add))
                g.dve_steps.wait(dve)
                pm = pmax.rearrange("p (m a) -> p m a", m=2)
                for tt in range(TT):
                    g.dve_steps.mark(dve.tensor_reduce(pm[:, :, tt], pb[h % 2][:, :, segs[tt]], AX.X, ALU.max))
                g.dve_steps.wait(dve)
                dve.tensor_scalar(mx[:, 4 * h:4 * h + 4], pmax, -scale, None, ALU.mult).then_inc(s_mk, 1)
                dve.wait_ge(s_mk, h + 1)

            masked(0)
            for h in range(HT):
                if h + 1 < HT:
                    masked(h + 1)
                dve.wait_ge(s_p, 4 * h + 4)
                c = cf[:, 4 * h:4 * h + 4]
                link(dve, dve.reciprocal(c, rowsum[:, 4 * h:4 * h + 4]))
                link(dve, dve.tensor_scalar(c[:, 2:4], c[:, 2:4], lam[:, 5:6], None, ALU.mult))
                if h >= 2:
                    dve.wait_ge(s_tr, h - 1)
                for tt in range(TT):
                    g.dve_steps.mark(dve.tensor_scalar(attn[h % 2][:, segs[tt]], pb[h % 2][:, 1, segs[tt]],
                                                       c[:, 2 + tt:3 + tt], None, ALU.mult))
                g.dve_steps.wait(dve)
                for tt in range(TT):
                    ins = dve.scalar_tensor_tensor(out=attn[h % 2][:, segs[tt]], in0=pb[h % 2][:, 0, segs[tt]],
                                                   scalar=c[:, tt:tt + 1], in1=attn[h % 2][:, segs[tt]],
                                                   op0=ALU.mult, op1=ALU.add)
                    if tt == 0:
                        g.dve_steps.mark(ins)
                    else:
                        ins.then_inc(s_at, 1)
                g.dve_steps.wait(dve)
            dve.wait_ge(s_oe, TT)
            link(dve, dve.tensor_tensor(osq, osb, osb, ALU.mult))
            link(dve, dve.tensor_reduce(oss, osq.rearrange("p (g e) -> p g e", e=P), AX.X, ALU.add))
            dve.tensor_scalar(omean, oss, 1.0 / P, SUB_EPS, ALU.mult, ALU.add).then_inc(s_om, 1)
            link(dve, dve.tensor_scalar(subln, subln, 1.0 - lam_init, None, ALU.mult))
            dve.wait_ge(s_or, 1)
            link(dve, dve.reciprocal(orstd, oroot))
            o8 = osb.rearrange("p (g e) -> p g e", e=P)
            link(dve, dve.tensor_tensor(o8, o8, orstd.unsqueeze(2).to_broadcast([P, 2 * HT, P]), ALU.mult))
            for tt in range(TT):
                g.dve_steps.mark(dve.tensor_tensor(g.mixn[:, tt, 0:HALF].rearrange("p (g e) -> p g e", e=P),
                                                   o8[:, HT * tt:HT * tt + HT, :],
                                                   subln.unsqueeze(1).to_broadcast([P, HT, P]), ALU.mult))
            g.dve_steps.wait(dve)

        @block.tensor
        def _(pe):
            n_pe(pe)
            n_ready(pe)
            for j in range(8):
                ch, half = divmod(j, 2)
                bank = ps[4 + j % 4]
                if j >= 4:
                    pe.wait_ge(s_ev, j - 3)
                if ch < 3:
                    ins = project_natural(g, pe, c0 + ch, g.hT, bank[:, :], half, slice(0, 512))
                else:
                    w = g.chunk(pe, c0 + ch)
                    for i in range(2):
                        n = (2 * half + i) * P
                        for k in range(KT):
                            ins = pe.matmul(bank[:, i * S:(i + 1) * S], w[:, k, n:n + P], g.hT[:, k, :],
                                            start=(k == 0), stop=(k == KT - 1))
                ins.then_inc(s_prj, 1)
            pe.wait_ge(s_qk, 4)
            for b in range(4):
                pe.wait_ge(s_ev, b + 5)
                for kk in range(2):
                    for tt in range(TT):
                        j = 2 * b + kk
                        ins = pe.transpose(ps[4 + b][:, kk * S + tt * P:kk * S + tt * P + P], qk[:, tt, j * P:(j + 1) * P], ident)
                ins.then_inc(s_qt, 1)
            pe.wait_ge(s_qT, 4)

            def scores(h):
                if h >= 2:
                    pe.wait_ge(s_mk, h - 1)
                for m in range(2):
                    r = slice(DH * m, DH * m + DH)
                    bank = ps[2 * (h % 2) + m]
                    pe.matmul(bank[:, 0:P], qkT[r, h, 0:P], qkT[r, HT + h, 0:P], start=True, stop=True)
                    ins = pe.matmul(bank[:, P:W3], qkT[r, h, P:S], qkT[r, HT + h, :], start=True, stop=True)
                ins.then_inc(s_sc, 1)

            scores(0)
            scores(1)
            for h in range(HT):
                pe.wait_ge(s_at, h + 1)
                if h >= 2:
                    pe.wait_ge(s_trc, h - 1)
                for j in range(3):
                    ins = pe.transpose(ps[4 + h % 2][:, j * P:(j + 1) * P], attn[h % 2][:, j * P:(j + 1) * P], ident)
                ins.then_inc(s_tr, 1)
                if h + 2 < HT:
                    scores(h + 2)
                pe.wait_ge(s_trc, h + 1)
                hs = slice(h * P, (h + 1) * P)
                v = attnT[h % 2]
                pe.matmul(ps[6][:, hs], v[:, 0:P], vn[:, 0, hs], start=True, stop=True)
                pe.matmul(ps[7][:, hs], v[:, P:S], vn[:, 0, hs], start=True, stop=False)
                pe.matmul(ps[7][:, hs], v[:, S:W3], vn[:, 1, hs], start=False, stop=True).then_inc(s_o, 1)

    col = lambda i: sm[:, 16 * i + 64:16 * i + 80]
    step, rho, turn, kk_, ths, thc, sn0, cs0, fr, fi, mod2, t0, t1, t2 = (col(i) for i in range(14))
    half_pi = sm[:, 400:401]
    quad = lambda i: work[:, 1024 * i:1024 * (i + 1)].rearrange("p (q t) -> p q t", q=4)
    frac = quad(0)
    kq = flat3(vn).rearrange("p (q t) -> p q t", q=4)
    sn, cs = [quad(1), g.mixT[:, 0:4, :]], [quad(2), g.mixT[:, 4:8, :]]
    Wz = [quad(3), quad(4)]
    mixn_quad = lambda i: g.xs[:, i, :].rearrange("p (q t) -> p q t", q=4)
    X1, X2 = [quad(5), quad(6)], [quad(7), mixn_quad(0)]
    xr, xi = mixn_quad(1), g.hT[:, 4:8, :]
    c_tmp = g.hT[:, 0:4, :].rearrange("p a t -> p (a t)")
    yT = uT
    zT = g.hT[:, 0:4, :]
    sig = g.xs[:, 0, :].rearrange("p (q t) -> p q t", q=4)
    MAGIC = 1.5 * 2 ** 23
    TWO_PI = 2 * np.pi
    PI_A = float(np.float32(6.28125))
    PI_B = float(np.float32(TWO_PI - PI_A))
    SIN_SCALE = 6.283184
    s_st, s_ac, s_th, s_sc2 = g.sem("s5_step_in"), g.sem("s5_step"), g.sem("s5_theta"), g.sem("s5_sin_cos")
    s_hp, s_c = g.sem("s5_constants"), g.sem("s5_c_scaled")
    s_fr, s_tab, s_abs = g.sem("s5_angles"), g.sem("s5_tables"), g.sem("s5_abs")
    s_bu, s_x1, s_x2, s_x, s_y, s_ye = (g.sem("s5_" + n) for n in (
        "Bu", "turned_back", "turned", "states", "y", "y_copied"))
    s_ge, s_gl, s_sg = g.sem("s5_gelu"), g.sem("s5_glu"), g.sem("s5_glu_sigmoid")
    g.free_when[c0 + 4] = (s_gl, 2)
    with nc.Block() as block:
        @block.gpsimd
        def _(pool):
            link = g.pool_steps.link
            pool.wait_ge(s_th, 1)
            for b in range(4):
                if b:
                    pool.wait_ge(s_tab, 2 * b)
                tm = con["time"].unsqueeze(1).to_broadcast([P, 4, S])
                link(pool, pool.tensor_tensor(frac, tm, turn[:, 4 * b:4 * b + 4].unsqueeze(2).to_broadcast([P, 4, S]), ALU.mult))
                link(pool, pool.tensor_scalar(kq, frac, MAGIC, None, ALU.add))
                link(pool, pool.tensor_scalar(kq, kq, MAGIC, None, ALU.subtract))
                pool.tensor_tensor(frac, frac, kq, ALU.subtract).then_inc(s_fr, 1)
                pool.wait_ge(s_fr, b + 1)

        @block.scalar
        def _(act):
            act.activation(step, lstep, ACT.Exp).then_inc(s_ac, 1)
            act.wait_ge(s_st, 1)
            act.activation(rho, t0, ACT.Exp).then_inc(s_ac, 1)
            act.wait_ge(s_th, 1)
            act.wait_ge(s_hp, 1)
            act.activation(sn0, turn, ACT.Sin, scale=SIN_SCALE).then_inc(s_sc2, 1)
            g.act_steps.link(act, act.activation(thc, turn, ACT.Abs))
            act.activation(cs0, thc, ACT.Sin, scale=-SIN_SCALE, bias=half_pi).then_inc(s_sc2, 1)
            for b in range(4):
                act.wait_ge(s_fr, b + 1)
                if b >= 2:
                    act.wait_ge(s_x2, b - 1)
                act.activation(sn[b % 2], frac, ACT.Sin, scale=SIN_SCALE).then_inc(s_tab, 1)
                g.act_steps.link(act, act.activation(cs[b % 2], frac, ACT.Abs))
                act.activation(cs[b % 2], cs[b % 2], ACT.Sin, scale=-SIN_SCALE, bias=half_pi).then_inc(s_tab, 1)
                act.wait_ge(s_tab, 2 * b + 2)
            for ctile in range(HT):
                act.wait_ge(s_ye, ctile + 1)
                act.activation(zT[:, ctile, :], yT[:, ctile, :], ACT.Gelu_apprx_tanh).then_inc(s_ge, 1)
            for q in range(2):
                act.wait_ge(s_gl, q + 1)
                act.activation(sig[:, 2 * q:2 * q + 2, :], bank2(ps[q]), ACT.Sigmoid).then_inc(s_sg, 1)

        @block.vector
        def _(dve):
            link = g.dve_steps.link
            dve.memset(half_pi, float(np.pi / 2)).then_inc(s_hp, 1)
            link(dve, dve.tensor_scalar(a_re, a_re, -1e-4, None, ALU.min))
            dve.wait_ge(s_ac, 1)
            dve.tensor_tensor(t0, a_re, step, ALU.mult).then_inc(s_st, 1)
            link(dve, dve.tensor_tensor(t1, a_im, step, ALU.mult))
            link(dve, dve.tensor_scalar(kk_, t1, 1.0 / TWO_PI, MAGIC, ALU.mult, ALU.add))
            link(dve, dve.tensor_scalar(kk_, kk_, MAGIC, None, ALU.subtract))
            link(dve, dve.scalar_tensor_tensor(out=t1, in0=kk_, scalar=-PI_A, in1=t1, op0=ALU.mult, op1=ALU.add))
            link(dve, dve.scalar_tensor_tensor(out=t1, in0=kk_, scalar=-PI_B, in1=t1, op0=ALU.mult, op1=ALU.add))
            link(dve, dve.tensor_scalar(turn, t1, 1.0 / TWO_PI, 0.5, ALU.mult, ALU.min))
            dve.tensor_scalar(turn, turn, -0.5, None, ALU.max).then_inc(s_th, 1)
            dve.wait_ge(s_ac, 2)
            dve.wait_ge(s_sc2, 2)
            link(dve, dve.tensor_tensor(t0, rho, cs0, ALU.mult))
            link(dve, dve.tensor_scalar(t0, t0, -1.0, None, ALU.add))
            link(dve, dve.tensor_tensor(t1, rho, sn0, ALU.mult))
            link(dve, dve.tensor_tensor(mod2, a_re, a_re, ALU.mult))
            link(dve, dve.tensor_tensor(t2, a_im, a_im, ALU.mult))
            link(dve, dve.tensor_tensor(mod2, mod2, t2, ALU.add))
            link(dve, dve.reciprocal(mod2, mod2))
            link(dve, dve.tensor_tensor(fr, t0, a_re, ALU.mult))
            link(dve, dve.tensor_tensor(t2, t1, a_im, ALU.mult))
            link(dve, dve.tensor_tensor(fr, fr, t2, ALU.add))
            link(dve, dve.tensor_tensor(fr, fr, mod2, ALU.mult))
            link(dve, dve.tensor_tensor(fi, t1, a_re, ALU.mult))
            link(dve, dve.tensor_tensor(t2, t0, a_im, ALU.mult))
            link(dve, dve.tensor_tensor(fi, fi, t2, ALU.subtract))
            link(dve, dve.tensor_tensor(fi, fi, mod2, ALU.mult))
            fb = lambda f: f.unsqueeze(2).to_broadcast([P, NPAIR, 2 * SC])
            ta, tb = (c_tmp[:, 512 * i:512 * (i + 1)].rearrange("p (q c) -> p q c", q=NPAIR) for i in range(2))
            g.dve_steps.mark(dve.tensor_tensor(ta, ct[:, 0], fb(fi), ALU.mult))
            g.dve_steps.mark(dve.tensor_tensor(tb, ct[:, 1], fb(fi), ALU.mult))
            link(dve, dve.tensor_tensor(ct[:, 0], ct[:, 0], fb(fr), ALU.mult))
            link(dve, dve.tensor_tensor(ct[:, 1], ct[:, 1], fb(fr), ALU.mult))
            link(dve, dve.tensor_tensor(ct[:, 0], ct[:, 0], tb, ALU.subtract))
            link(dve, dve.tensor_tensor(ct[:, 1], ct[:, 1], ta, ALU.add))
            dve.tensor_scalar(ct[:, 1], ct[:, 1], -1.0, None, ALU.mult).then_inc(s_c, 1)
            for b in range(4):
                dve.wait_ge(s_tab, 2 * b + 2)
                if b:
                    dve.wait_ge(s_x, 2 * b)
                for i in range(4):
                    dve.wait_ge(s_bu, 4 * b + i + 1)
                    bu = bank2(ps[i])
                    for X, tab in ((X1, cs[b % 2]), (X2, sn[b % 2])):
                        for ri in range(2):
                            ins = dve.tensor_tensor(X[ri][:, i, :], bu[:, ri, :], tab[:, i, :], ALU.mult)
                            if i == 3 and X is X2 and ri == 1:
                                ins.then_inc(s_x1, 1)
                            else:
                                g.dve_steps.mark(ins)
                g.dve_steps.wait(dve)
                dve.wait_ge(s_x1, b + 1)
                g.dve_steps.mark(dve.tensor_tensor(Wz[0], X1[0], X2[1], ALU.add))
                g.dve_steps.mark(dve.tensor_tensor(Wz[1], X1[1], X2[0], ALU.subtract))
                g.dve_steps.wait(dve)
                for ri in range(2):
                    for i in range(4):
                        q = 4 * b + i
                        g.dve_steps.mark(dve.tensor_tensor_scan(Wz[ri][:, i, :], rho[:, q:q + 1].to_broadcast([P, S]),
                                                                Wz[ri][:, i, :], 0.0, ALU.mult, ALU.add))
                g.dve_steps.wait(dve)
                for X, tab in ((X1, cs[b % 2]), (X2, sn[b % 2])):
                    for ri in range(2):
                        ins = dve.tensor_tensor(X[ri], Wz[ri], tab, ALU.mult)
                        if X is X2 and ri == 1:
                            ins.then_inc(s_x2, 1)
                        else:
                            g.dve_steps.mark(ins)
                g.dve_steps.wait(dve)
                dve.wait_ge(s_x2, b + 1)
                if b:
                    dve.wait_ge(s_y, b)
                dve.tensor_tensor(xr, X1[0], X2[1], ALU.subtract).then_inc(s_x, 1)
                dve.tensor_tensor(xi, X1[1], X2[0], ALU.add).then_inc(s_x, 1)
            for ctile in range(HT):
                dve.wait_ge(s_y, ctile + 1)
                src = ps[4 + ctile][:, 0:S]
                dve.scalar_tensor_tensor(out=yT[:, ctile, :], in0=uT[:, ctile, :], scalar=dcol[:, ctile:ctile + 1], in1=src,
                                         op0=ALU.mult, op1=ALU.add).then_inc(s_ye, 1)
            for q in range(2):
                dve.wait_ge(s_sg, q + 1)
                g.dve_steps.mark(dve.tensor_tensor(g.mixT[:, 4 + 2 * q:6 + 2 * q, :], zT[:, 2 * q:2 * q + 2, :],
                                                   sig[:, 2 * q:2 * q + 2, :], ALU.mult))
            g.dve_steps.wait(dve)

        @block.tensor
        def _(pe):
            def inputs(b):
                for i in range(4):
                    r = slice(32 * i, 32 * i + 32)
                    if b:
                        pe.wait_ge(s_x1, b)
                    for ri in range(2):
                        ins = pe.matmul(ps[i][:, ri * S:(ri + 1) * S], bt[r, ri, b, :], uT[r, b, :], start=True, stop=True,
                                        tile_position=(32 * i, 0))
                    ins.then_inc(s_bu, 1)

            inputs(0)
            pe.wait_ge(s_c, 1)
            for b in range(4):
                if b < 3:
                    inputs(b + 1)
                pe.wait_ge(s_x, 2 * b + 2)
                for i in range(4):
                    o = ps[4 + b][32 * i:32 * i + 32, 0:S]
                    pe.matmul(o, ct[:, 0, 4 * b + i, :], xr[:, i, :], start=True, stop=False, tile_position=(0, 32 * i))
                    ins = pe.matmul(o, ct[:, 1, 4 * b + i, :], xi[:, i, :], start=False, stop=True, tile_position=(0, 32 * i))
                ins.then_inc(s_y, 1)
            pe.wait_ge(s_ge, HT)
            w = g.chunk(pe, c0 + 4)
            for q in range(2):
                for i in range(2):
                    n = (2 * q + i) * P
                    for k in range(HT):
                        ins = pe.matmul(ps[q][:, i * S:(i + 1) * S], w[:, k, n:n + P], zT[:, k, :],
                                        start=(k == 0), stop=(k == HT - 1))
                ins.then_inc(s_gl, 1)

    output_projection(g, "odd", c0 + 5, [0, 1, 2, 3], 1)
    g.end_phase()
    return c0 + 7


def moe_layer(g, ly, c0):
    nc, A, ps = g.nc, g.A, g.ps
    n_ = f"moe{ly}_"
    g.at = 0
    ident = g.con("ident")
    gcol = g.take(KT)
    wr = g.take(KT * 36).rearrange("p (k n) -> p k n", n=36)
    brow = g.take(36)
    lg = g.take(TT * 36).rearrange("p (a n) -> p a n", a=TT)
    ge = lambda: g.take(TT * NE).rearrange("p (a n) -> p a n", a=TT)
    e1, oh1, oh2, w1, gate, sel, rankm = (ge() for _ in range(7))
    oh4 = g.take(TT * NG).rearrange("p (a n) -> p a n", a=TT)
    g4 = g.take(TT * NG).rearrange("p (a n) -> p a n", a=TT)
    v4 = g.take(TT * NG).rearrange("p (a n) -> p a n", a=TT)
    cnt = g.take(NE)
    zeros = g.take(512)
    Pm = [g.take(TT * P).rearrange("p (a j) -> p a j", a=TT) for _ in range(2)]
    Pg = [g.take(TT * P).rearrange("p (a j) -> p a j", a=TT) for _ in range(2)]
    PT = [g.take(S) for _ in range(2)]
    xg = [g.take(KT * CAP).rearrange("p (k j) -> p k j", k=KT) for _ in range(2)]
    sil = [g.take(HID) for _ in range(2)]
    hid = [g.take(HID) for _ in range(2)]
    hidT = [g.take(4 * CAP).rearrange("p (f j) -> p f j", f=4) for _ in range(2)]
    y = [g.take(512) for _ in range(2)]
    sm = g.small
    c2 = lambda at: sm[:, at:at + 2]
    u2 = lambda ap, n: ap.unsqueeze(2).to_broadcast([P, TT, n])
    s_gain = g.sem(n_ + "gain_landed")
    n_act, n_dve, n_pe, n_ready = stage_norm(g, n_ + "in", gcol, s_gain)
    s_par = g.sem(n_ + "params_landed")
    s_lg, s_gd, s_ex = g.sem(n_ + "logits"), g.sem(n_ + "exp_in"), g.sem(n_ + "exp")
    s_sel, s_rk, s_reps = g.sem(n_ + "selected"), g.sem(n_ + "ranks"), g.sem(n_ + "turns")
    with nc.Block() as block:
        @block.sync
        def _(sp):
            sp.dma_start(gcol, A["moe_norm_g"][ly]).then_inc(s_gain, 16)
            sp.dma_start(wr[:, :, 0:NG], A["moe_w_group"][ly].rearrange("(k p) n -> p k n", p=P)).then_inc(s_par, 16)
            sp.dma_start(wr[:, :, NG:], A["moe_w_expert"][ly].rearrange("(k p) n -> p k n", p=P)).then_inc(s_par, 16)
            sp.dma_start(brow[:, 0:NG], A["moe_b_group"][ly].partition_broadcast(P)).then_inc(s_par, 16)
            sp.dma_start(brow[:, NG:], A["moe_b_expert"][ly].partition_broadcast(P)).then_inc(s_par, 16)

        @block.scalar
        def _(act):
            n_act(act)
            act.wait_ge(s_gd, 1)
            act.activation(v4, g4, ACT.Exp).then_inc(s_ex, 1)
            act.wait_ge(s_gd, 2)
            act.activation(c2(320), c2(318), ACT.Exp).then_inc(s_ex, 1)

        @block.vector
        def _(dve):
            link = g.dve_steps.link
            iota = lambda n: g.con("iota_e")[:, 0:n].unsqueeze(1).to_broadcast([P, TT, n])

            def first_max(vals, mx, n, onehot, cand):
                link(dve, dve.tensor_reduce(mx, vals, AX.X, ALU.max))
                link(dve, dve.tensor_tensor(onehot, vals, u2(mx, n), ALU.is_ge))
                link(dve, dve.scalar_tensor_tensor(out=cand, in0=iota(n), scalar=-100.0, in1=onehot, op0=ALU.add, op1=ALU.mult))
                link(dve, dve.tensor_reduce(c2(300), cand, AX.X, ALU.min))
                link(dve, dve.tensor_scalar(c2(300), c2(300), 100.0, None, ALU.add))
                link(dve, dve.tensor_tensor(onehot, iota(n), u2(c2(300), n), ALU.is_equal))

            n_dve(dve)
            dve.wait_ge(s_par, 64)
            dve.wait_ge(s_lg, TT)
            for tt in range(TT):
                g.dve_steps.mark(dve.tensor_tensor(lg[:, tt, :], ps[4 + tt][:, 0:36], brow, ALU.add))
            g.dve_steps.wait(dve)
            first_max(lg[:, :, 0:NG], c2(302), NG, oh4, g4)
            dve.tensor_tensor(g4, lg[:, :, 0:NG], u2(c2(302), NG), ALU.subtract).then_inc(s_gd, 1)
            lge = lg[:, :, NG:].rearrange("p a (g e) -> p a g e", g=NG)
            e1v = e1.rearrange("p a (g e) -> p a g e", g=NG)
            w1v = w1.rearrange("p a (g e) -> p a g e", g=NG)
            for tt in range(TT):
                ohb = oh4[:, tt, :].unsqueeze(2).to_broadcast([P, NG, 8])
                g.dve_steps.mark(dve.tensor_scalar(w1v[:, tt], ohb, -NEG, NEG, ALU.mult, ALU.add))
                link(dve, dve.tensor_tensor(e1v[:, tt], lge[:, tt], ohb, ALU.mult))
            link(dve, dve.tensor_tensor(e1, e1, w1, ALU.add))
            first_max(e1, c2(304), NE, oh1, w1)
            link(dve, dve.scalar_tensor_tensor(out=e1, in0=oh1, scalar=2 * NEG, in1=e1, op0=ALU.mult, op1=ALU.add))
            first_max(e1, c2(306), NE, oh2, w1)
            dve.tensor_tensor(c2(318), c2(306), c2(304), ALU.subtract).then_inc(s_gd, 1)
            dve.tensor_tensor(sel, oh1, oh2, ALU.add).then_inc(s_sel, 1)
            dve.wait_ge(s_ex, 2)
            link(dve, dve.tensor_reduce(c2(308), v4, AX.X, ALU.add))
            link(dve, dve.reciprocal(c2(310), c2(308)))
            link(dve, dve.tensor_scalar(c2(312), c2(320), 1.0, None, ALU.add))
            link(dve, dve.reciprocal(c2(314), c2(312)))
            link(dve, dve.tensor_tensor(c2(314), c2(314), c2(310), ALU.mult))
            link(dve, dve.tensor_tensor(c2(316), c2(314), c2(320), ALU.mult))
            link(dve, dve.tensor_tensor(oh1, oh1, u2(c2(314), NE), ALU.mult))
            dve.wait_ge(s_sel, 1)
            link(dve, dve.tensor_tensor(oh2, oh2, u2(c2(316), NE), ALU.mult))
            link(dve, dve.tensor_tensor(gate, oh1, oh2, ALU.add))
            dve.wait_ge(s_rk, 1)
            pr = ps[4][:, 64:64 + TT * NE].rearrange("p (a n) -> p a n", a=TT)
            link(dve, dve.scalar_tensor_tensor(out=rankm, in0=pr, scalar=1.0, in1=sel, op0=ALU.add, op1=ALU.mult))
            link(dve, dve.tensor_scalar(rankm, rankm, -1.0, None, ALU.add))
            link(dve, dve.tensor_reduce(sm[:, 330:331], ps[4][:, 128:128 + NE], AX.X, ALU.max))
            for i in range(3):
                g.dve_steps.mark(dve.tensor_scalar(sm[:, 332 + i:333 + i], sm[:, 330:331], float(CAP * (i + 1)), None, ALU.is_gt))
            g.dve_steps.wait(dve)
            link(dve, dve.tensor_reduce(sm[:, 336:337], sm[:, 332:335], AX.X, ALU.add))
            link(dve, dve.tensor_scalar(g.turns[:, :], sm[:, 336:337], 1.0, None, ALU.add))
            link(dve, dve.memset(zeros, 0.0))

        @block.tensor
        def _(pe):
            n_pe(pe)
            n_ready(pe)
            pe.wait_ge(s_par, 64)
            for tt in range(TT):
                for k in range(KT):
                    ins = pe.matmul(ps[4 + tt][:, 0:36], g.hT[:, k, tt * P:(tt + 1) * P], wr[:, k, :],
                                    start=(k == 0), stop=(k == KT - 1))
                ins.then_inc(s_lg, 1)
            pe.wait_ge(s_sel, 1)
            before, ones = g.con("before"), g.con("ones")
            pe.matmul(ps[4][:, 64:64 + NE], before, sel[:, 0, :], start=True, stop=True)
            pe.matmul(ps[4][:, 64 + NE:64 + 2 * NE], ones, sel[:, 0, :], start=True, stop=False)
            pe.matmul(ps[4][:, 64 + NE:64 + 2 * NE], before, sel[:, 1, :], start=False, stop=True)
            pe.matmul(ps[4][:, 128:128 + NE], ones, sel[:, 0, :], start=True, stop=False)
            pe.matmul(ps[4][:, 128:128 + NE], ones, sel[:, 1, :], start=False, stop=True).then_inc(s_rk, 1)

    slot = lambda par, which: g.ring[:, (c0 + 3 * par + which) % SLOTS, :]
    landed = lambda par, which: g.moe_landed[ly][3 * par + which]
    wide = lambda par, which: slot(par, which).rearrange("p (k n) -> p k n", n=HID if which < 2 else D)
    s_P, s_Pt, s_PTc = g.sem(n_ + "P"), g.sem(n_ + "P_transposed"), g.sem(n_ + "P_copied")
    s_G, s_xg, s_gu, s_sl = g.sem(n_ + "gathered"), g.sem(n_ + "x_copied"), g.sem(n_ + "gate_up"), g.sem(n_ + "silu")
    s_h, s_ht, s_hc = g.sem(n_ + "hidden"), g.sem(n_ + "hidden_transposed"), g.sem(n_ + "hidden_copied")
    s_dn, s_yc, s_sc = g.sem(n_ + "down"), g.sem(n_ + "y_copied"), g.sem(n_ + "scattered")
    s_sub, s_pm, s_fin = g.sem(n_ + "ranks_lowered"), g.sem(n_ + "P_ungated"), g.sem(n_ + "sum_closed")
    STEPS = NE // 2
    turns = lambda eng: eng.value_load(g.turns[0:1, 0:1], min_val=1, max_val=S // CAP)
    with nc.Block() as block:
        @block.sync
        def _(sp):
            T = turns(sp)

            def load(par, e, step):
                for which, name in enumerate(("moe_w_gate", "moe_w_up", "moe_w_down")):
                    src = A[name][ly].rearrange("e (k p) n -> e p k n", p=P)[e]
                    sp.wait_ge(s_gu if which < 2 else s_dn, step * 2 + par + 1)
                    sp.dma_start(wide(par, which), src).then_inc(landed(par, which), 16)

            with sp.Fori(0, T) as t:
                with sp.Fori(0, STEPS - 1) as i:
                    for par in range(2):
                        load(par, i * 2 + (2 + par), t * STEPS + i)
                with sp.If(t < T - 1):
                    for par in range(2):
                        load(par, par, t * STEPS + (STEPS - 1))
            g.limit = len(g.chunks)
            if c0 < g.limit:
                sp.wait_ge(s_dn, T * NE)
                g.send(sp, c0 + SLOTS)

        @block.scalar
        def _(act):
            with act.Fori(0, turns(act)) as t:
                with act.Fori(0, STEPS) as i:
                    n2 = (t * STEPS + i) * 2
                    for par in range(2):
                        act.wait_ge(s_Pt, n2 + par + 1)
                        act.wait_ge(s_sc, n2 + par + 1)
                        act.copy(PT[par], ps[4 + par][:, 0:S]).then_inc(s_PTc, 1)
                    for par in range(2):
                        act.wait_ge(s_gu, n2 + par + 1)
                        act.activation(sil[par][0:CAP, :], ps[4 + par][0:CAP, :], ACT.Silu).then_inc(s_sl, 1)
                    for par in range(2):
                        act.wait_ge(s_ht, n2 + par + 1)
                        act.copy(hidT[par], ps[6 + par][:, 0:4 * CAP].rearrange("p (f j) -> p f j", f=4)).then_inc(s_hc, 1)
                    for par in range(2):
                        act.wait_ge(s_dn, n2 + par + 1)
                        act.copy(y[par], ps[4 + par][:, :]).then_inc(s_yc, 1)

        @block.vector
        def _(dve):
            with dve.Fori(0, turns(dve)) as t:
                with dve.Fori(0, STEPS) as i:
                    n2 = (t * STEPS + i) * 2
                    for par in range(2):
                        e = bass.ds(i * 2 + par, 1)
                        dve.tensor_tensor(Pm[par], g.con("iota").unsqueeze(1).to_broadcast([P, TT, P]),
                                          rankm[:, :, e].to_broadcast([P, TT, P]), ALU.is_equal).then_inc(s_pm, 1)
                        dve.wait_ge(s_pm, n2 + par + 1)
                        dve.tensor_tensor(Pg[par], Pm[par], gate[:, :, e].to_broadcast([P, TT, P]), ALU.mult).then_inc(s_P, 1)
                    for par in range(2):
                        dve.wait_ge(s_G, n2 + par + 1)
                        dve.tensor_tensor(xg[par], ps[6 + par][:, :].rearrange("p (k j) -> p k j", k=KT),
                                          gcol.unsqueeze(2).to_broadcast([P, KT, CAP]), ALU.mult).then_inc(s_xg, 1)
                    for par in range(2):
                        dve.wait_ge(s_sl, n2 + par + 1)
                        dve.tensor_tensor(hid[par][0:CAP, :], sil[par][0:CAP, :], ps[4 + par][CAP:2 * CAP, :], ALU.mult)\
                           .then_inc(s_h, 1)
                    dve.wait_ge(s_P, n2 + 2)
                dve.tensor_scalar(rankm, rankm, float(-CAP), None, ALU.add).then_inc(s_sub, 1)
                dve.wait_ge(s_sub, t + 1)
            dve.wait_ge(s_fin, 1)
            for j in range(4):
                v = g.x[:, j // 2, (j % 2) * 512:(j % 2 + 1) * 512]
                g.dve_steps.mark(dve.tensor_tensor(v, v, ps[j][:, :], ALU.add))
            g.dve_steps.wait(dve)

        @block.tensor
        def _(pe):
            for b in range(4):
                ins = pe.matmul(ps[b][:, :], zeros[:, 0:P], zeros, start=True, stop=False)
                if b % 2:
                    ins.then_inc(s_sc, 1)
            with pe.Fori(0, turns(pe)) as t:
                with pe.Fori(0, STEPS) as i:
                    n2 = (t * STEPS + i) * 2
                    for par in range(2):
                        pe.wait_ge(s_P, n2 + par + 1)
                        for tt in range(TT):
                            ins = pe.transpose(ps[4 + par][:, tt * P:(tt + 1) * P], Pg[par][:, tt, :], ident)
                        ins.then_inc(s_Pt, 1)
                    for par in range(2):
                        for k in range(KT):
                            for tt in range(TT):
                                ins = pe.matmul(ps[6 + par][:, k * CAP:(k + 1) * CAP], g.xs[:, tt, k * P:(k + 1) * P],
                                                Pm[par][:, tt, 0:CAP], start=(tt == 0), stop=(tt == TT - 1))
                        ins.then_inc(s_G, 1)
                    for par in range(2):
                        pe.wait_ge(s_xg, n2 + par + 1)
                        pe.wait_ge(s_PTc, n2 + par + 1)
                        for which in range(2):
                            pe.wait_ge(landed(par, which), (t * STEPS + i) * 16 + 16)
                        for k in range(KT):
                            for which in range(2):
                                ins = pe.matmul(ps[4 + par][which * CAP:(which + 1) * CAP, :], xg[par][:, k, :],
                                                wide(par, which)[:, k, :], start=(k == 0), stop=(k == KT - 1))
                        ins.then_inc(s_gu, 1)
                    for par in range(2):
                        pe.wait_ge(s_h, n2 + par + 1)
                        for f in range(4):
                            turn = pe.matmul if f == 0 else pe.transpose
                            ins = turn(ps[6 + par][:, f * CAP:(f + 1) * CAP], hid[par][0:CAP, f * P:(f + 1) * P],
                                       ident[0:CAP, 0:CAP])
                        ins.then_inc(s_ht, 1)
                        pe.wait_ge(s_hc, n2 + par + 1)
                        pe.wait_ge(landed(par, 2), (t * STEPS + i) * 16 + 16)
                        for f in range(4):
                            for nh in range(2):
                                ins = pe.matmul(ps[4 + par][nh * CAP:(nh + 1) * CAP, :], hidT[par][:, f, :],
                                                wide(par, 2)[:, f, nh * 512:(nh + 1) * 512], start=(f == 0), stop=(f == 3))
                        ins.then_inc(s_dn, 1)
                    for par in range(2):
                        pe.wait_ge(s_yc, n2 + par + 1)
                        for tt in range(TT):
                            for nh in range(2):
                                r = slice(nh * CAP, (nh + 1) * CAP)
                                ins = pe.matmul(ps[2 * tt + nh][:, :], PT[par][r, tt * P:(tt + 1) * P], y[par][r, :],
                                                start=False, stop=False, skip_group_check=True)
                        ins.then_inc(s_sc, 1)
            for b in range(4):
                ins = pe.matmul(ps[b][:, :], zeros[:, 0:P], zeros, start=False, stop=True)
            ins.then_inc(s_fin, 1)
    g.end_phase()


def moe_prefetch(g, sp, ly, c0):
    for m in range(SLOTS):
        par, which = divmod(m, 3)
        if c0 + m - SLOTS in g.free_when:
            sp.wait_ge(*g.free_when[c0 + m - SLOTS])
        src = g.A[("moe_w_gate", "moe_w_up", "moe_w_down")[which]][ly, par].rearrange("(k p) n -> p k n", p=P)
        dst = g.ring[:, (c0 + m) % SLOTS, :].rearrange("p (k n) -> p k n", n=HID if which < 2 else D)
        sp.dma_start(dst, src).then_inc(g.moe_landed[ly][m], 16)


def weight_plan(g):
    A, chunks = g.A, g.chunks

    def add(w, cols, kt):
        chunks.append((w[:, cols[0]:cols[1]].rearrange("(k p) n -> p k n", p=P), kt, cols[1] - cols[0]))

    for l in range(DEPTH):
        for c in IN_ORDER:
            add(A["w_in"][l], (c * 512, c * 512 + 512), KT)
        for c in range(2):
            add(A["w_out"][l], (c * 512, c * 512 + 512), KT)
        add(A["w_ple"][l], (0, D), 2)
        for c in range(2):
            add(A["w_ple_gate"][l], (c * 512, c * 512 + 512), KT)
    for c in range(3):
        add(A["even_w_in"][0], (c * 512, c * 512 + 512), KT)
    add(A["even_w_in"][0], (1536, 1792), KT)
    add(A["even_w_in"][0], (1792, 2304), KT)
    for c in range(2):
        add(A["even_w_out"][0], (c * 512, c * 512 + 512), KT)
    g.limit = len(chunks)
    for c in range(4):
        add(A["odd_w_in"][0], (c * 512, c * 512 + 512), KT)
    add(A["s5_w_glu"][0], (0, HALF), HT)
    for c in range(2):
        add(A["odd_w_out"][0], (c * 512, c * 512 + 512), KT)


def setup(g):
    nc, A, ps = g.nc, g.A, g.ps
    n_first = sum(n for _, n in g.where_first.values())
    at, n_oh = g.where_first["buckets"]
    g.first_consts = g.arena[:, g.arena_size - n_first:]
    g.moba_bias = g.arena[:, g.arena_size - n_first - 4 * 384:g.arena_size - n_first]
    table = g.arena[:, 0:4]
    tables = g.arena[:, 8:8 + 4 * P].rearrange("p (h m) -> p h m", h=4)
    rows = g.arena[:, 1024:1024 + 4 * 511].rearrange("p (h j) -> p h j", h=4)
    scratch = nc.dram_tensor("bias_rows", (4, P, 511), F32).ap()
    s_c, s_x, s_m, s_t = g.sem("constants_landed"), g.sem("x_landed"), g.sem("table_masked"), g.sem("tables_spread")
    s_r, s_rc, s_w, s_b = g.sem("bias_rows"), g.sem("bias_rows_copied"), g.sem("bias_rows_written"), g.sem("bias_landed")
    with nc.Block() as block:
        @block.sync
        def _(sp):
            sp.dma_start(g.x[:, :, :], A["x"][0].rearrange("(a p) n -> p a n", p=P)).then_inc(s_x, 16)
            sp.wait_ge(s_m, 1)
            sp.dma_start(table[0:BUCKETS, :], A["rel_bias"]).then_inc(s_c, 16)
            sp.dma_start(g.first_consts, A["c_first"]).then_inc(s_c, 16)
            sp.dma_start(g.res[:, :], A["c_res"]).then_inc(s_c, 16)
            g.send(sp, 2)
            sp.wait_ge(s_x, 16)

        @block.vector
        def _(dve):
            dve.memset(table[:, :], NEG).then_inc(s_m, 1)
            dve.wait_ge(s_c, 48)
            dve.tensor_copy(tables, table.unsqueeze(2).to_broadcast([P, 4, P])).then_inc(s_t, 1)

        @block.tensor
        def _(pe):
            pe.wait_ge(s_t, 1)
            for h in range(4):
                pe.matmul(ps[h][:, 0:511], tables[0:64, h, :], g.first_consts[0:64, at:at + n_oh], start=True, stop=True)\
                  .then_inc(s_r, 1)

        @block.scalar
        def _(act):
            for h in range(4):
                act.wait_ge(s_r, h + 1)
                act.copy(rows[:, h, :], ps[h][:, 0:511]).then_inc(s_rc, 1)
                act.wait_ge(s_rc, h + 1)
                act.dma_start(scratch[h], rows[:, h, :]).then_inc(s_w, 16)
            act.wait_ge(s_w, 64)
            for h in range(4):
                for tt in range(TT):
                    src = bass.AP(scratch.tensor, h * P * 511 + 255 - tt * P, [[510, P], [1, (tt + 1) * P]])
                    dst = g.moba_bias[:, h * 384 + tt * P:h * 384 + tt * P + (tt + 1) * P]
                    act.dma_start(dst, src).then_inc(s_b, 16)
            act.wait_ge(s_b, 16 * 8)
    g.end_phase()


def write_out(g):
    with g.nc.Block() as block:
        @block.sync
        def _(sp):
            sp.dma_start(g.out[0].rearrange("(a p) n -> p a n", p=P), g.x[:, :, :]).then_inc(g.out_written, 16)
            sp.wait_ge(g.out_written, 16)


def build(nc, A, out, wheres):
    with ExitStack() as ctx:
        g = Program(nc, A, out, wheres, ctx)
        weight_plan(g)
        setup(g)
        c = 0
        for l in range(DEPTH):
            c = first_layer(g, l, c)
        c = even_layer(g, c)
        moe_layer(g, 0, c)
        c = odd_layer(g, c)
        moe_layer(g, 1, c)
        write_out(g)


def laid_out(inputs):
    a = {k: np.asarray(v) for k, v in inputs.items()}
    r = {k: a[k] for k in ("x", "p", "w_in", "ret_norm_g", "q_norm_g", "k_norm_g", "rel_bias", "w_out", "w_ple",
                           "ple_norm_g", "w_ple_gate")}
    cols = lambda v: np.ascontiguousarray(v.reshape(v.shape[0], -1, P).transpose(0, 2, 1))
    r["norm_g"] = cols(a["norm_g"])
    r["even_norm_g"] = cols(a["norm_mix_g_2"])[0]
    for k in ("rw_mu", "rw_w0", "rw_a0", "rw_k_k", "rw_k_a", "pool_scale"):
        r[k] = cols(a[k + "_2"])[0]
    r["rw_r_k"] = cols(a["rw_r_k_2"].reshape(1, -1))[0]
    r["moe_norm_g"] = cols(a["norm_ffn_g_2"])
    r["odd_norm_g"] = cols(a["norm_mix_g_2"])[1]
    r["s5_d"] = cols(a["s5_d_2"].reshape(1, -1))[0]
    for k in ("s5_a_re", "s5_a_im", "s5_log_step"):
        r[k] = a[k + "_2"].reshape(NPAIR, P).T
    b = np.zeros((HT, 4, 2, SC, 2, 2, SP_), np.float32)
    c = np.zeros((2, SP_, 2, NPAIR, 2, SC), np.float32)
    for ri, (kb, kc) in enumerate((("s5_b_re_2", "s5_c_re_2"), ("s5_b_im_2", "s5_c_im_2"))):
        vb = a[kb][0].reshape(HT, 4, 2, SP_, SC)
        vc = a[kc][0].reshape(NPAIR, 2, SC, SP_)
        for i in range(2):
            b[:, :, i, :, ri, i, :] = vb[:, :, i].transpose(0, 1, 3, 2)
            c[i, :, ri, :, i, :] = vc[:, i].transpose(2, 0, 1)
    r["s5_b"] = b.transpose(1, 2, 3, 4, 0, 5, 6).reshape(P, 2, HT, P)
    r["s5_c"] = c.reshape(P, 2, NPAIR, 2 * SC)
    for k in ("odd_w_in", "odd_w_out", "da_q_norm", "da_k_norm", "da_subln", "da_lam_q1", "da_lam_q2", "da_lam_k1",
              "da_lam_k2", "s5_w_glu", "moe_w_group", "moe_b_group", "moe_w_expert", "moe_b_expert", "moe_w_gate", "moe_w_up", "moe_w_down",
              "even_w_in", "even_w_out", "rw_w2", "rw_a2", "rw_g2", "rw_ln_g", "rw_ln_b", "pool_w"):
        r[k] = a[k + "_2"]
    return r


def kernel(**inputs):
    import concourse.bacc as _bacc
    from concourse.bass_utils import run_bass_kernel_spmd as _run

    nc = _bacc.Bacc("TRN2", target_bir_lowering=False, num_devices=1)
    arrays = laid_out(inputs)
    wheres = []
    for name, consts in zip(("c_res", "c_first", "c_even", "c_odd"), shape_constants()):
        arrays[name], where = packed(consts)
        wheres.append(where)
    A = {}
    feed = {}
    for name, a in arrays.items():
        feed[f"in_{name}"] = np.ascontiguousarray(a)
        A[name] = nc.dram_tensor(f"in_{name}", a.shape, mybir.dt.from_np(a.dtype), kind="ExternalInput").ap()
    out = nc.dram_tensor("out", (1, S, D), F32, kind="ExternalOutput").ap()
    build(nc, A, out, wheres)
    r = _run(nc, [feed], core_ids=[0])
    return r.results[0]["out"]
```
